# Optimizing a Trainium2 kernel written in Bass

```python
import jax, jax.numpy as jnp
from jax import lax
import numpy as np
import jax
import jax.numpy as jnp

D_MODEL = 1024
BATCH = 1
SEQ = 512
DEPTH = 1

HEAD_DIM = 64
NSA_HEADS = 8
NSA_KV_HEADS = 2
SWA_HEADS = 8
SWA_KV_HEADS = 2
N_HEADS = NSA_HEADS + SWA_HEADS
MIX_WIDTH = N_HEADS * HEAD_DIM
CMP_LEN = 32
CMP_STRIDE = 16
CMP_HIDDEN = 128
SEL_LEN = 64
N_SEL = 16
NSA_WINDOW = 512
NSA_Q_BLOCK = 64
SWA_WINDOW = 128
SWA_Q_BLOCK = 128
D_FF = 2816
CONV_W = 3
PLE_DIM = 256
RMS_EPS = 1e-6
NEG_INF = -1e30
FORCE_BONUS = 1e6

NSA_Q_W = NSA_HEADS * HEAD_DIM
NSA_KV_W = NSA_KV_HEADS * HEAD_DIM
NSA_GATE_W = 3 * NSA_HEADS
SWA_Q_W = SWA_HEADS * HEAD_DIM
SWA_KV_W = SWA_KV_HEADS * HEAD_DIM
IN_SPLITS = [NSA_Q_W] + [NSA_KV_W] * 6 + [NSA_GATE_W, SWA_Q_W, SWA_KV_W, SWA_KV_W]
IN_WIDTH = sum(IN_SPLITS)
IN_SPLIT_POINTS = [int(v) for v in np.cumsum(IN_SPLITS)[:-1]]


def rmsnorm(x, g):
    xf = x.astype(jnp.float32)
    y = xf * lax.rsqrt(jnp.mean(xf * xf, axis=-1, keepdims=True) + RMS_EPS)
    return (y * g.astype(jnp.float32)).astype(x.dtype)

def alibi_slopes():
    h = jnp.arange(N_HEADS, dtype=jnp.float32)
    return jnp.exp2(-8.0 * (h + 1.0) / N_HEADS)

def compress_kv(kv, pe, w1, w2):
    B, S, G, hd = kv.shape
    r = CMP_LEN // CMP_STRIDE
    seg = kv.reshape(B, S // CMP_STRIDE, CMP_STRIDE, G, hd)
    n_cmp = S // CMP_STRIDE - r + 1
    blocks = jnp.concatenate([seg[:, i:i + n_cmp] for i in range(r)], axis=2)
    blocks = blocks + pe.astype(kv.dtype)[:, None, :]
    flat = jnp.transpose(blocks, (0, 1, 3, 2, 4)).reshape(B, n_cmp, G, CMP_LEN * hd)
    hid = jax.nn.gelu(flat @ w1.astype(kv.dtype))
    return hid @ w2.astype(kv.dtype)

def nsa_attention(q, k_cmp, v_cmp, k_slc, v_slc, k_win, v_win, gates, slopes):
    B, S, H, hd = q.shape
    G = k_slc.shape[2]
    R = H // G
    C = NSA_Q_BLOCK
    n_cmp = k_cmp.shape[1]
    n_sb = S // SEL_LEN
    n_top = min(N_SEL, n_sb)
    scale = hd ** -0.5
    slopes_g = slopes.reshape(G, R)
    cmp_start = jnp.arange(n_cmp) * CMP_STRIDE
    cmp_end = cmp_start + CMP_LEN - 1
    sel_start = jnp.arange(n_sb) * SEL_LEN
    overlap = ((cmp_start[:, None] < sel_start[None, :] + SEL_LEN)
               & (cmp_end[:, None] >= sel_start[None, :])).astype(jnp.float32)
    kb = jnp.transpose(k_slc.reshape(B, n_sb, SEL_LEN, G, hd), (0, 3, 1, 2, 4))
    vb = jnp.transpose(v_slc.reshape(B, n_sb, SEL_LEN, G, hd), (0, 3, 1, 2, 4))
    pad = ((0, 0), (NSA_WINDOW, 0), (0, 0), (0, 0))
    k_wp = jnp.pad(k_win, pad)
    v_wp = jnp.pad(v_win, pad)
    bi = jnp.arange(B)[:, None, None, None]
    gi = jnp.arange(G)[None, :, None, None]
    blk = jnp.arange(n_sb)

    def one_block(c):
        t0 = c * C
        t = t0 + jnp.arange(C)
        qc = lax.dynamic_slice_in_dim(q, t0, C, axis=1).reshape(B, C, G, R, hd)
        gc = lax.dynamic_slice_in_dim(gates, t0, C, axis=1).reshape(B, C, G, R, 3)
        dist_c = (t[:, None] - cmp_end[None, :]).astype(jnp.float32)
        valid_c = dist_c >= 0
        s_c = jnp.einsum('bcgrd,bngd->bgrcn', qc, k_cmp).astype(jnp.float32) * scale
        s_c = jnp.where(valid_c, s_c - slopes_g[:, :, None, None] * dist_c, NEG_INF)
        p_c = jax.nn.softmax(s_c, axis=-1) * valid_c
        o_c = jnp.einsum('bgrcn,bngd->bcgrd', p_c.astype(v_cmp.dtype), v_cmp)
        imp = jnp.einsum('bgrcn,nj->bgcj', p_c, overlap)
        jt = t // SEL_LEN
        forced = (blk[None, :] == 0) | (blk[None, :] == jt[:, None]) | (blk[None, :] == jt[:, None] - 1)
        imp = jnp.where(forced, FORCE_BONUS, imp)
        imp = jnp.where(blk[None, :] <= jt[:, None], imp, NEG_INF)
        _, idx = lax.top_k(imp, n_top)
        ks = kb[bi, gi, idx]
        vs = vb[bi, gi, idx]
        pos = idx[..., None] * SEL_LEN + jnp.arange(SEL_LEN)
        dist_s = (t[:, None, None] - pos).astype(jnp.float32)[:, :, None]
        s_s = jnp.einsum('bcgrd,bgcnld->bgrcnl', qc, ks).astype(jnp.float32) * scale
        s_s = jnp.where(dist_s >= 0, s_s - slopes_g[None, :, :, None, None, None] * dist_s, NEG_INF)
        p_s = jax.nn.softmax(s_s, axis=(-2, -1))
        o_s = jnp.einsum('bgrcnl,bgcnld->bcgrd', p_s.astype(vs.dtype), vs)
        kw = lax.dynamic_slice_in_dim(k_wp, t0, C + NSA_WINDOW, axis=1)
        vw = lax.dynamic_slice_in_dim(v_wp, t0, C + NSA_WINDOW, axis=1)
        s_pos = t0 - NSA_WINDOW + jnp.arange(C + NSA_WINDOW)
        dist_w = t[:, None] - s_pos[None, :]
        valid_w = (dist_w >= 0) & (dist_w < NSA_WINDOW) & (s_pos[None, :] >= 0)
        s_w = jnp.einsum('bcgrd,bkgd->bgrck', qc, kw).astype(jnp.float32) * scale
        s_w = jnp.where(valid_w, s_w - slopes_g[:, :, None, None] * dist_w.astype(jnp.float32), NEG_INF)
        p_w = jax.nn.softmax(s_w, axis=-1)
        o_w = jnp.einsum('bgrck,bkgd->bcgrd', p_w.astype(vw.dtype), vw)
        o = gc[..., 0:1] * o_c + gc[..., 1:2] * o_s + gc[..., 2:3] * o_w
        return o.reshape(B, C, H * hd)

    out = lax.map(one_block, jnp.arange(S // C))
    return jnp.transpose(out, (1, 0, 2, 3)).reshape(B, S, H * hd)

def swa_attention(q, k, v, sinks, slopes):
    B, S, H, hd = q.shape
    G = k.shape[2]
    R = H // G
    C = SWA_Q_BLOCK
    n_q = S // C
    scale = hd ** -0.5
    qb = q.reshape(B, n_q, C, G, R, hd)
    pad = ((0, 0), (C, 0), (0, 0), (0, 0))
    kp = jnp.pad(k, pad).reshape(B, n_q + 1, C, G, hd)
    vp = jnp.pad(v, pad).reshape(B, n_q + 1, C, G, hd)
    kb = jnp.concatenate([kp[:, :-1], kp[:, 1:]], axis=2)
    vb = jnp.concatenate([vp[:, :-1], vp[:, 1:]], axis=2)
    i = jnp.arange(C)[:, None]
    j = jnp.arange(2 * C)[None, :]
    dist = C + i - j
    kpos = jnp.arange(n_q)[:, None, None] * C - C + j[None]
    valid = (dist >= 0) & (dist < SWA_WINDOW) & (kpos >= 0)
    slopes_g = slopes.reshape(G, R)
    s = jnp.einsum('bnqgrd,bnkgd->bngrqk', qb, kb).astype(jnp.float32) * scale
    s = s - slopes_g[:, :, None, None] * dist.astype(jnp.float32)
    s = jnp.where(valid[:, None, None], s, NEG_INF)
    sg = sinks.astype(jnp.float32).reshape(G, R)[:, :, None, None]
    m = jnp.maximum(jnp.max(s, axis=-1, keepdims=True), sg)
    e = jnp.exp(s - m)
    prob = e / (jnp.sum(e, axis=-1, keepdims=True) + jnp.exp(sg - m))
    o = jnp.einsum('bngrqk,bnkgd->bnqgrd', prob.astype(vb.dtype), vb)
    return o.reshape(B, S, H * hd)

def causal_dwconv(a, w, b):
    y = lax.conv_general_dilated(a, w[:, None, :].astype(a.dtype), window_strides=(1,),
                                 padding=[(CONV_W - 1, 0)],
                                 dimension_numbers=('NWC', 'WIO', 'NWC'),
                                 feature_group_count=a.shape[-1])
    return y + b.astype(a.dtype)

def first_inputs(seed: int = 0) -> dict:
    key = jax.random.key(seed)
    ks = jax.random.split(key, 24)
    f32 = jnp.float32
    L = DEPTH

    def nrm(k, shape, scale):
        return jax.random.normal(k, shape, f32) * scale

    def gain(k):
        return 1.0 + 0.02 * jax.random.normal(k, (L, D_MODEL), f32)

    return {
        'x': nrm(ks[0], (BATCH, SEQ, D_MODEL), 1.0),
        'p': nrm(ks[1], (DEPTH, BATCH, SEQ, PLE_DIM), 1.0),
        'attn_pre_g': gain(ks[2]),
        'w_in': nrm(ks[3], (L, D_MODEL, IN_WIDTH), D_MODEL ** -0.5),
        'cmp_pe_k': nrm(ks[4], (L, CMP_LEN, HEAD_DIM), 0.02),
        'cmp_w1_k': nrm(ks[5], (L, CMP_LEN * HEAD_DIM, CMP_HIDDEN), (CMP_LEN * HEAD_DIM) ** -0.5),
        'cmp_w2_k': nrm(ks[6], (L, CMP_HIDDEN, HEAD_DIM), CMP_HIDDEN ** -0.5),
        'cmp_pe_v': nrm(ks[7], (L, CMP_LEN, HEAD_DIM), 0.02),
        'cmp_w1_v': nrm(ks[8], (L, CMP_LEN * HEAD_DIM, CMP_HIDDEN), (CMP_LEN * HEAD_DIM) ** -0.5),
        'cmp_w2_v': nrm(ks[9], (L, CMP_HIDDEN, HEAD_DIM), CMP_HIDDEN ** -0.5),
        'sinks': nrm(ks[10], (L, SWA_HEADS), 1.0),
        'w_o': nrm(ks[11], (L, MIX_WIDTH, D_MODEL), MIX_WIDTH ** -0.5),
        'attn_post_g': gain(ks[12]),
        'mlp_pre_g': gain(ks[13]),
        'w_gate_up': nrm(ks[14], (L, D_MODEL, 2 * D_FF), D_MODEL ** -0.5),
        'conv_w': nrm(ks[15], (L, CONV_W, D_FF), CONV_W ** -0.5),
        'conv_b': nrm(ks[16], (L, D_FF), 0.01),
        'w_down': nrm(ks[17], (L, D_FF, D_MODEL), D_FF ** -0.5),
        'mlp_post_g': gain(ks[18]),
        'w_ple': nrm(ks[19], (L, PLE_DIM, D_MODEL), PLE_DIM ** -0.5),
        'w_ple_gate': nrm(ks[20], (L, D_MODEL, D_MODEL), D_MODEL ** -0.5),
    }

def first_block(x, p, attn_pre_g, w_in, cmp_pe_k, cmp_w1_k, cmp_w2_k, cmp_pe_v, cmp_w1_v, cmp_w2_v,
              sinks, w_o, attn_post_g, mlp_pre_g, w_gate_up, conv_w, conv_b, w_down, mlp_post_g,
              w_ple, w_ple_gate):
    B, S, _ = x.shape
    slopes = alibi_slopes()
    swa_slopes = slopes[:SWA_HEADS]
    nsa_slopes = slopes[SWA_HEADS:]
    for i in range(DEPTH):
        h = rmsnorm(x, attn_pre_g[i])
        proj = h @ w_in[i].astype(h.dtype)
        (q_n, kc, vc, ksl, vsl, kwn, vwn, g_n, q_s, k_s, v_s) = jnp.split(proj, IN_SPLIT_POINTS, axis=-1)
        kv_shape = (B, S, NSA_KV_HEADS, HEAD_DIM)
        k_cmp = compress_kv(kc.reshape(kv_shape), cmp_pe_k[i], cmp_w1_k[i], cmp_w2_k[i])
        v_cmp = compress_kv(vc.reshape(kv_shape), cmp_pe_v[i], cmp_w1_v[i], cmp_w2_v[i])
        gates = jax.nn.sigmoid(g_n).reshape(B, S, NSA_HEADS, 3)
        o_nsa = nsa_attention(q_n.reshape(B, S, NSA_HEADS, HEAD_DIM), k_cmp, v_cmp,
                              ksl.reshape(kv_shape), vsl.reshape(kv_shape),
                              kwn.reshape(kv_shape), vwn.reshape(kv_shape), gates, nsa_slopes)
        o_swa = swa_attention(q_s.reshape(B, S, SWA_HEADS, HEAD_DIM),
                              k_s.reshape(B, S, SWA_KV_HEADS, HEAD_DIM),
                              v_s.reshape(B, S, SWA_KV_HEADS, HEAD_DIM), sinks[i], swa_slopes)
        mix = jnp.concatenate([o_nsa, o_swa], axis=-1) @ w_o[i].astype(x.dtype)
        x = x + rmsnorm(mix, attn_post_g[i])
        h = rmsnorm(x, mlp_pre_g[i])
        gu = h @ w_gate_up[i].astype(h.dtype)
        a, u = jnp.split(gu, [D_FF], axis=-1)
        a = causal_dwconv(a, conv_w[i], conv_b[i])
        y = (jax.nn.gelu(a, approximate=True) * u) @ w_down[i].astype(h.dtype)
        x = x + rmsnorm(y, mlp_post_g[i])
        e = p[i] @ w_ple[i].astype(x.dtype)
        x = x + e * jax.nn.sigmoid(x @ w_ple_gate[i].astype(x.dtype))
    return x


DEPTH_2 = 2

CHUNK = 64
N_META = 16
N_HEADS_A = 8
D_A = N_HEADS_A * HEAD_DIM
N_IDX_HEADS = 8
IDX_DIM = HEAD_DIM
TOPK_MAX = 256
POOL_WINDOWS = (2, 4, 8, 16)
N_POOL_GROUPS = len(POOL_WINDOWS)
D_B = D_MODEL // 2
POOL_GROUP_DIM = D_B // N_POOL_GROUPS
Q_BLOCK = 128
ROPE_THETA = 10000.0
EPS = 1e-6
NEG_INF_2 = -1e30
IN_WIDTHS = (D_A, HEAD_DIM, HEAD_DIM, D_A, D_B, D_B, N_IDX_HEADS * IDX_DIM, IDX_DIM, N_IDX_HEADS, 2 * D_MODEL)
D_IN = sum(IN_WIDTHS)


def rms_norm(x, g):
    xf = x.astype(jnp.float32)
    y = xf * lax.rsqrt(jnp.mean(xf * xf, axis=-1, keepdims=True) + EPS)
    return (y * g.astype(jnp.float32)).astype(x.dtype)

def rope_tables(length, dim):
    inv_freq = 1.0 / (ROPE_THETA ** (jnp.arange(0, dim, 2, dtype=jnp.float32) / dim))
    ang = jnp.arange(length, dtype=jnp.float32)[:, None] * inv_freq[None, :]
    ang = jnp.concatenate([ang, ang], axis=-1)
    return jnp.cos(ang), jnp.sin(ang)

def apply_rope(x, cos, sin):
    half = x.shape[-1] // 2
    xf = x.astype(jnp.float32)
    rot = jnp.concatenate([-xf[..., half:], xf[..., :half]], axis=-1)
    return (xf * cos + rot * sin).astype(x.dtype)

def chunk_id(pos):
    return jnp.where(pos < N_META, 0, 1 + (pos - N_META) // CHUNK)

def indexer_sparse_attention(q, k, v, q_idx, k_idx, w_idx, k_top):
    B, T = q.shape[0], q.shape[1]
    n_blk = -(-T // Q_BLOCK)
    t_pad = n_blk * Q_BLOCK

    def to_blocks(a):
        a = jnp.pad(a, [(0, 0), (0, t_pad - T)] + [(0, 0)] * (a.ndim - 2))
        return jnp.moveaxis(a.reshape((B, n_blk, Q_BLOCK) + a.shape[2:]), 1, 0)

    key_chunk = chunk_id(jnp.arange(T))
    query_chunk = chunk_id(jnp.arange(t_pad)).reshape(n_blk, Q_BLOCK)
    k_idx_f = k_idx.astype(jnp.float32)
    idx_scale = (N_IDX_HEADS ** -0.5) * (IDX_DIM ** -0.5)
    attn_scale = HEAD_DIM ** -0.5
    gather = jax.vmap(lambda table, ids: table[ids])

    def one_block(args):
        qb, qib, wib, qcb = args
        s = jnp.einsum('bqhd,bkd->bqhk', qib.astype(jnp.float32), k_idx_f)
        score = jnp.einsum('bqhk,bqh->bqk', jax.nn.relu(s), wib.astype(jnp.float32) * idx_scale)
        visible = key_chunk[None, :] <= qcb[:, None]
        score = jnp.where(visible[None], score, NEG_INF_2)
        _, sel = lax.top_k(score, k_top)
        valid = key_chunk[sel] <= qcb[None, :, None]
        kg = gather(k, sel)
        vg = gather(v, sel)
        logits = jnp.einsum('bqhd,bqkd->bqhk', qb, kg).astype(jnp.float32) * attn_scale
        logits = jnp.where(valid[:, :, None, :], logits, NEG_INF_2)
        p = jax.nn.softmax(logits, axis=-1).astype(vg.dtype)
        return jnp.einsum('bqhk,bqkd->bqhd', p, vg)

    out = lax.map(one_block, (to_blocks(q), to_blocks(q_idx), to_blocks(w_idx), query_chunk))
    return jnp.moveaxis(out, 0, 1).reshape(B, t_pad, N_HEADS_A, HEAD_DIM)[:, :T]

def multiscale_pool(u, pool_w, pool_b, pool_s):
    B, T, C = u.shape
    G = POOL_GROUP_DIM
    uf = u.astype(jnp.float32)
    cs = jnp.concatenate([jnp.zeros((B, 1, C), jnp.float32), jnp.cumsum(uf, axis=1)], axis=1)
    t1 = jnp.arange(1, T + 1, dtype=jnp.float32)
    means = []
    for g, w in enumerate(POOL_WINDOWS):
        csg = cs[..., g * G:(g + 1) * G]
        lag = jnp.concatenate([jnp.zeros((B, w, G), jnp.float32), csg[:, :T + 1 - w]], axis=1)
        cnt = jnp.minimum(t1, float(w))
        means.append((csg[:, 1:] - lag[:, 1:]) / cnt[None, :, None])
    pooled = (jnp.concatenate(means, axis=-1) - uf).astype(u.dtype).reshape(B, T, N_POOL_GROUPS, G)
    mixed = jnp.einsum('btgc,gcd->btgd', pooled, pool_w) + pool_b.reshape(N_POOL_GROUPS, G)
    return mixed.reshape(B, T, C) * pool_s

def hybrid_layer(x, norm_g, w_in, qn_g, kn_g, pool_w, pool_b, pool_s, w_a, w_b, w_out, cos, sin, k_top):
    B, T, _ = x.shape
    h = rms_norm(x, norm_g)
    proj = jnp.einsum('btd,de->bte', h, w_in)
    q, k, v, gate_a, u_b, gate_b, q_idx, k_idx, w_idx, merge = jnp.split(
        proj, np.cumsum(IN_WIDTHS)[:-1].tolist(), axis=-1)
    cos_h, sin_h = cos[:, None, :], sin[:, None, :]
    q = apply_rope(rms_norm(q.reshape(B, T, N_HEADS_A, HEAD_DIM), qn_g), cos_h, sin_h)
    k = apply_rope(rms_norm(k, kn_g), cos, sin)
    q_idx = apply_rope(q_idx.reshape(B, T, N_IDX_HEADS, IDX_DIM), cos_h, sin_h)
    k_idx = apply_rope(k_idx, cos, sin)
    attn = indexer_sparse_attention(q, k, v, q_idx, k_idx, w_idx, k_top).reshape(B, T, D_A)
    y_a = jnp.einsum('bte,ed->btd', attn * jax.nn.silu(gate_a), w_a)
    pooled = multiscale_pool(u_b, pool_w, pool_b, pool_s)
    y_b = jnp.einsum('bte,ed->btd', pooled * jax.nn.silu(gate_b), w_b)
    g_a, g_b = jnp.split(jax.nn.sigmoid(merge), 2, axis=-1)
    return x + jnp.einsum('btd,de->bte', g_a * y_a + g_b * y_b, w_out)

def second_inputs(seed: int = 0) -> dict:
    key = jax.random.key(seed)
    ks = jax.random.split(key, 12)

    def nrm(k, shape, scale):
        return scale * jax.random.normal(k, shape, jnp.float32)

    return {
        'x': nrm(ks[0], (BATCH, SEQ, D_MODEL), 1.0),
        'meta_tokens': nrm(ks[1], (N_META, D_MODEL), 1.0),
        'norm_gain': 1.0 + nrm(ks[2], (DEPTH_2, D_MODEL), 0.05),
        'w_in': nrm(ks[3], (DEPTH_2, D_MODEL, D_IN), D_MODEL ** -0.5),
        'q_norm_gain': 1.0 + nrm(ks[4], (DEPTH_2, HEAD_DIM), 0.05),
        'k_norm_gain': 1.0 + nrm(ks[5], (DEPTH_2, HEAD_DIM), 0.05),
        'pool_w': nrm(ks[6], (DEPTH_2, N_POOL_GROUPS, POOL_GROUP_DIM, POOL_GROUP_DIM), POOL_GROUP_DIM ** -0.5),
        'pool_b': nrm(ks[7], (DEPTH_2, D_B), 0.02),
        'pool_scale': 1.0 + nrm(ks[8], (DEPTH_2, D_B), 0.1),
        'w_branch_a': nrm(ks[9], (DEPTH_2, D_A, D_MODEL), D_A ** -0.5),
        'w_branch_b': nrm(ks[10], (DEPTH_2, D_B, D_MODEL), D_B ** -0.5),
        'w_out': nrm(ks[11], (DEPTH_2, D_MODEL, D_MODEL), D_MODEL ** -0.5),
    }

def second_block(x, meta_tokens, norm_gain, w_in, q_norm_gain, k_norm_gain, pool_w, pool_b, pool_scale,
              w_branch_a, w_branch_b, w_out):
    B, S, _ = x.shape
    k_top = min(TOPK_MAX, S // 4)
    meta = jnp.broadcast_to(meta_tokens.astype(x.dtype)[None], (B, N_META, D_MODEL))
    h = jnp.concatenate([meta, x], axis=1)
    T = S + N_META
    cos, sin = rope_tables(T, HEAD_DIM)
    for l in range(DEPTH_2):
        h = hybrid_layer(h, norm_gain[l], w_in[l], q_norm_gain[l], k_norm_gain[l], pool_w[l], pool_b[l],
                         pool_scale[l], w_branch_a[l], w_branch_b[l], w_out[l], cos, sin, k_top)
    return h[:, N_META:]


def setup_inputs(seed=0):
    out = dict(first_inputs(seed))
    for name, value in second_inputs(seed + 1).items():
        if name != "x":
            out[name + "_2"] = value
    return out


def reference(
    x, p, attn_pre_g, w_in, cmp_pe_k, cmp_w1_k, cmp_w2_k, cmp_pe_v, cmp_w1_v, cmp_w2_v, sinks,
    w_o, attn_post_g, mlp_pre_g, w_gate_up, conv_w, conv_b, w_down, mlp_post_g, w_ple,
    w_ple_gate, meta_tokens_2, norm_gain_2, w_in_2, q_norm_gain_2, k_norm_gain_2, pool_w_2,
    pool_b_2, pool_scale_2, w_branch_a_2, w_branch_b_2, w_out_2,
):
    x = first_block(
        x, p, attn_pre_g, w_in, cmp_pe_k, cmp_w1_k, cmp_w2_k, cmp_pe_v, cmp_w1_v, cmp_w2_v,
        sinks, w_o, attn_post_g, mlp_pre_g, w_gate_up, conv_w, conv_b, w_down, mlp_post_g,
        w_ple, w_ple_gate,
    )
    return second_block(
        x, meta_tokens_2, norm_gain_2, w_in_2, q_norm_gain_2, k_norm_gain_2, pool_w_2, pool_b_2,
        pool_scale_2, w_branch_a_2, w_branch_b_2, w_out_2,
    )


_drawn_inputs = setup_inputs


def setup_inputs(seed=0):
    import zlib

    import numpy as np

    out = dict(_drawn_inputs(seed))
    spreads = {}
    factors = {'cmp_pe_k': 8.0,
     'cmp_pe_v': 5.604,
     'attn_post_g': 3.424,
     'mlp_pre_g': 3.224,
     'conv_b': 8.0,
     'mlp_post_g': 4.817,
     'meta_tokens_2': 4.492,
     'norm_gain_2': 3.274,
     'q_norm_gain_2': 8.0,
     'k_norm_gain_2': 8.0,
     'pool_b_2': 8.0}
    for name, (base, spread) in spreads.items():
        noise = np.random.default_rng([zlib.crc32(name.encode()), seed]).standard_normal(out[name].shape)
        drawn = base * np.exp(spread * noise) if base else spread * noise
        out[name] = jnp.asarray(drawn.astype(out[name].dtype))
    for name, factor in factors.items():
        out[name] = (out[name] * factor).astype(out[name].dtype)
    return out
```

```python
from contextlib import ExitStack

import numpy as np

import concourse.bass as bass
import concourse.mybir as mybir

F32 = mybir.dt.float32
F32R = mybir.dt.float32r
ALU = mybir.AluOpType
ACT = mybir.ActivationFunctionType

P = 128
D = 1024
DC = D // P
S = 512
META = 16
T = S + META
TH = T // 2
HD = 64
QT = S // P
HEADS = 8
GROUPS = 2
REP = 4
NCMP = 31
CMP_STRIDE = 16
FC = 2816 // P
PLE_C = 2
LAYERS = 2
POOL_C = 4
TOPK = 128
EPS = 1e-6
SCALE = HD ** -0.5
BIG = 1e30
GELU_A = 0.7978845608028654
GELU_B = 0.044715

U_KC, U_VC, U_KSL, U_KWN, U_KS, U_VSL, U_VWN, U_VS, U_Q = 0, 1, 2, 3, 4, 5, 6, 7, 8
U_WO = 16
U_GU = U_WO + DC
U_DOWN = U_GU + 2 * FC
U_PLE = U_DOWN + FC
U_LAYER = U_PLE + DC + PLE_C
L_K, L_V, L_QI, L_Q, L_GA, L_POOL, L_MERGE, L_WAB, L_OUT = 0, 1, 2, 6, 10, 14, 22, 38, 46
L_UNITS = 54
UNITS = U_LAYER + LAYERS * L_UNITS

C_ID, C_ONES, C_BONES, C_ROT = 0, P, 2 * P, 3 * P
C_COS = 4 * P
C_SIN = C_COS + T
C_DIST = C_SIN + T
C_SDIST = C_DIST + S
C_CDIST = C_SDIST + 2 * P
C_SOME = C_CDIST + QT * 32
C_CNT = C_SOME + QT
C_VIS = C_CNT + POOL_C * META
C_EPS = C_VIS + HD
NC_CONST = C_EPS + 1

V_PRE, V_POST, V_MPRE, V_MPOST = 0, DC, 2 * DC, 3 * DC
V_CONVW = 4 * DC
V_CONVB = V_CONVW + 3 * FC
V_PEK = V_CONVB + FC
V_PEV = V_PEK + 16
V_SINK = V_PEV + 16
NC_VEC = V_SINK + HEADS

W_NORM, W_QN, W_KN, W_PB, W_PS = 0, DC, DC + 1, DC + 2, DC + 2 + POOL_C
NC_LVEC = DC + 2 + 2 * POOL_C


def slope(h):
    return 2.0 ** (-8.0 * (h + 1) / 16)


class Tally:

    def __init__(self, nc, ctx, known):
        self.nc, self.ctx, self.known = nc, ctx, known
        self.sems, self.count, self.events, self.gains = {}, {}, {}, {}
        self.loop = self.i = None
        self.trips = {}

    def sem(self, name):
        if name not in self.sems:
            self.sems[name] = self.ctx.enter_context(self.nc.semaphore(name))
        return self.sems[name]

    def tick(self, name, key, n=1):
        self.count[name] = self.count.get(name, 0) + n
        assert (name, key) not in self.events, (name, key)
        self.events[name, key] = (self.count[name], self.loop)
        return self.sem(name), n

    def at(self, name, key):
        if self.known is None:
            return self.sem(name), 1
        value, loop = self.known.events[name, key]
        if loop is not None:
            gain = self.known.gains[name, loop]
            if loop == self.loop:
                value = value + self.i * gain
            else:
                value = value + (self.known.trips[loop] - 1) * gain
        return self.sem(name), value

    def enter(self, loop, i, trips):
        self.loop, self.i, self.before = loop, i, dict(self.count)
        self.trips[loop] = trips

    def leave(self):
        for name, n in self.count.items():
            gain = n - self.before.get(name, 0)
            if gain:
                self.gains[name, self.loop] = gain
                self.count[name] += gain * (self.trips[self.loop] - 1)
        self.loop = self.i = None


def build(nc, io, known):
    ctx = ExitStack()
    with ctx:
        ty = Tally(nc, ctx, known)
        tick, at = ty.tick, ty.at

        def sb(name, shape, dt=F32, scope=ctx):
            return scope.enter_context(nc.sbuf_tensor(name, shape, dt))

        const = sb("const", [P, NC_CONST])
        vec = sb("vec", [P, NC_VEC])
        lvec = sb("lvec", [P, NC_LVEC])
        x = sb("x", [P, DC, T])
        hh = sb("hh", [P, DC, T], F32R)
        hl = sb("hl", [P, DC, T], F32R)
        raw = [sb(f"raw{s}", [P, DC, P]) for s in range(2)]
        whi = [sb(f"whi{s}", [P, DC, P], F32R) for s in range(2)]
        wlo = [sb(f"wlo{s}", [P, DC, P], F32R) for s in range(2)]
        pts = sb("pts", [P, 2, REP * P])
        small = sb("small", [P, 16, 8])

        scope = ExitStack()
        probs = sb("probs", [P, 2, REP, T], F32, scope)
        tmp = sb("tmp", [P, 4, T], F32, scope)
        rstd = sb("rstd", [P, T], F32, scope)
        both = ExitStack()
        q1 = sb("q1", [P, 8, S], F32, both)
        k1 = {n: sb(f"k1_{n}", [P, GROUPS, S], F32, both) for n in ("slc", "win", "swa")}
        v1 = {n: sb(f"v1_{n}", [P, QT, P], F32, both) for n in ("slc", "win", "swa")}
        seg = {n: sb(f"seg_{n}", [P, GROUPS, S], F32, both) for n in "kv"}
        cw1 = {n: sb(f"cw1_{n}", [P, 16, P], F32, both) for n in "kv"}
        cw2 = {n: sb(f"cw2_{n}", [P, P], F32, both) for n in "kv"}
        hid = {n: sb(f"hid_{n}", [P, 4, 62], F32, both) for n in "kv"}
        pecol = sb("pecol", [P, 2], F32, both)
        kcmp = sb("kcmp", [P, GROUPS, NCMP], F32, both)
        vcmp = sb("vcmp", [NCMP, GROUPS, HD], F32, both)
        bias1 = sb("bias1", [P, HEADS, S], F32, both)
        wg = sb("wg", [P, DC, 24], F32, both)
        wgh = sb("wgh", [P, DC, 24], F32R, both)
        wgl = sb("wgl", [P, DC, 24], F32R, both)
        gates = sb("gates", [P, 3, QT, 24], F32, both)
        mixf = sb("mixf", [P, 2, P], F32, both)
        both.close()
        mlp = ExitStack()
        acth = sb("acth", [P, FC, S], F32R, mlp)
        actl = sb("actl", [P, FC, S], F32R, mlp)
        mlp.close()
        ple = ExitStack()
        pT = sb("pT", [P, PLE_C, S], F32, ple)
        ph = sb("ph", [P, PLE_C, S], F32R, ple)
        pl = sb("pl", [P, PLE_C, S], F32R, ple)
        ple.close()
        scope.close()
        q2 = sb("q2", [P, 4, T])
        qi2 = sb("qi2", [P, 4, T])
        kT2 = sb("kT2", [P, T])
        kiT2 = sb("kiT2", [P, T])
        v2 = sb("v2", [P, QT + 1, 72])
        poolw = sb("poolw", [P, POOL_C, P])
        ah = sb("ah", [P, 4, T], F32R)
        al = sb("al", [P, 4, T], F32R)
        bh = sb("bh", [P, 4, T], F32R)
        bl = sb("bl", [P, 4, T], F32R)
        merge = sb("merge", [P, 2 * DC, T])
        probs2 = sb("probs2", [P, REP, T])
        sila = sb("sila", [P, 4, T])
        pool3 = merge[:, 12:2 * DC, :].rearrange("p c t -> p (c t)")[:, 0:3 * (META + T)]\
            .rearrange("p (s t) -> p s t", s=3)
        gateb = merge[:, 11, :]
        score = sb("score", [P, 2, T])
        keep = sb("keep", [P, T])
        relu = sb("relu", [P, 2, T])
        top8 = sb("top8", [P, 8])
        rq = sb("rq", [P, 3, QT + 1, 8])

        PS = [ctx.enter_context(nc.psum_tensor(f"ps{n}", [P, 2, 512], F32)) for n in range(4)]
        G, S0, S1, X = PS

        def pooled(c):
            return pool3[:, 2 - c % 2, META:META + T]

        ident = const[:, C_ID:C_ID + P]
        ones = const[:, C_ONES:C_ONES + P]
        bones = const[:, C_BONES:C_BONES + P]
        rot = const[:, C_ROT:C_ROT + P]
        eps = const[:, C_EPS:C_EPS + 1]

        def full(ps):
            return ps[:, :, 0:TH]

        def halves(ap):
            return ap.rearrange("p (a t) -> p a t", a=2)

        jobs1 = [(kind, g, t) for g in range(GROUPS) for t in range(QT) for kind in ("cmp", "slc", "win")]
        jobs1 += [("swa", g, t) for g in range(GROUPS) for t in range(QT)]

        def span1(kind, t):
            if kind == "cmp":
                return 0, NCMP
            if kind == "swa":
                lo = max(t - 1, 0) * P
                return lo, (t + 1) * P - lo
            return 0, (t + 1) * P

        def blocks1(kind, t):
            lo, n = span1(kind, t)
            return [(lo + b * P, min(P, n - b * P)) for b in range(-(-n // P))]

        def last_of_output(kind):
            return kind in ("win", "swa")

        def rows2(j):
            return (0, META) if j == 0 else (META + (j - 1) * P, P)

        def seen2(j):
            return META + j * P

        def parts2(n):
            return [(0, n)] if n <= 512 else [(0, TH), (TH, n - TH)]

        def scores2(ps, m, n):
            return ps[0:m, 0, 0:n] if n <= 512 else ps[0:m, :, 0:TH]

        def wide(ap, n):
            return ap if n <= 512 else ap.rearrange("p (a t) -> p a t", a=2)

        jobs2 = [(j, half) for j in range(QT + 1) for half in range(2)]
        filler = {j: [] for j in range(QT + 1)}
        order = [("ga", c) for c in range(4)]
        for c in range(4):
            order += [("gb", c), ("ub", c)]
        order += [("mg", c) for c in range(2 * DC)]
        for n, u in enumerate(order):
            filler[min(n * (QT + 1) // len(order), QT)].append(u)

        bank_of, turns2 = {}, {}
        count = -1
        for j in range(QT + 1):
            uses = [("relued", (j, h)) for h in range(HEADS) if j]
            uses += [("masked", (j, half, r)) for half in range(2) for r in range(REP)]
            for use in uses:
                bank_of[use] = len(bank_of) % 2
            for half in range(2):
                turns2[j, half] = count
                count += j + 1
        turns2[QT + 1, 0] = count

        def unit_of(kind, c):
            return {"gb": L_POOL + 2 * c, "ub": L_POOL + 2 * c + 1, "ga": L_GA + c, "mg": L_MERGE + c}[kind]

        block = ctx.enter_context(nc.Block())

        def hold(eng):
            eng.sem_inc(ty.sem("held"), 1)

        def unit_ready(n):
            return n + 1

        @block.sync
        def _(sp):
            sp.dma_start(x[:, :, META:T], io["x"]).then_inc(*tick("x_in", 0, 16))
            sp.dma_start(const[:], io["const"]).then_inc(*tick("const_in", 0, 16))
            sp.dma_start(vec[:], io["vec"]).then_inc(*tick("vec_in", 0, 16))
            for s in range(2):
                sp.dma_start(raw[s][:], io["w"][s]).then_inc(*tick(f"raw_in{s}", "first", 16))
            sp.dma_start(x[:, :, 0:META], io["meta"]).then_inc(*tick("meta_in", 0, 16))
            sp.dma_start(wg[:], io["wg"]).then_inc(*tick("wg_in", 0, 16))
            for n in "kv":
                sp.dma_start(cw1[n][:], io["cw1" + n]).then_inc(*tick(f"cw_in_{n}", 1, 16))
                sp.dma_start(cw2[n][:], io["cw2" + n]).then_inc(*tick(f"cw_in_{n}", 2, 16))
            with sp.Fori(1, UNITS // 2) as i:
                for s in range(2):
                    sp.wait_ge(ty.sem("unit_split"), 2 * i + s - 1)
                    sp.dma_start(raw[s][:], io["w"][2 * i + s]).then_inc(ty.sem(f"raw_in{s}"), 16)
            sp.wait_ge(*at("x_new", ("layer", DC - 1)))
            sp.dma_start(io["out"], x[:, :, META:T]).then_inc(*tick("out_stored", 0, 16))
            sp.wait_ge(*at("out_stored", 0))

        @block.gpsimd
        def _(pool):
            def split(i, s, first):
                if not first:
                    pool.wait_ge(ty.sem("unit_used"), 2 * i + s - 1)
                pool.wait_ge(ty.sem(f"raw_in{s}"), 16 * i + 16)
                hold(pool)
                pool.tensor_scalar(whi[s][:], raw[s][:], 1.0, 0.0, ALU.mult, ALU.add)\
                    .then_inc(ty.sem("unit_high"), 1)
                pool.wait_ge(ty.sem("unit_high"), 2 * i + s + 1)
                pool.tensor_tensor(wlo[s][:], raw[s][:], whi[s][:].bitcast(F32), ALU.subtract)\
                    .then_inc(ty.sem("unit_split"), 1)

            for s in range(2):
                split(0, s, True)
            with pool.Fori(1, UNITS // 2) as i:
                for s in range(2):
                    split(i, s, False)

        @block.tensor
        def _(pe):
            def three(out, wh, wl, ah_, al_, start, stop, flip=False):
                mm = None
                for n, (w, a) in enumerate(((wh, ah_), (wh, al_), (wl, ah_))):
                    lhs, rhs = (a, w) if flip else (w, a)
                    mm = pe.matmul(out, lhs, rhs, start=start and n == 0, stop=stop and n == 2)
                return mm

            def unit(n, slot, outs, chunks):
                pe.wait_ge(ty.sem("unit_split"), unit_ready(n))
                for k, out, ah_, al_, start, stop in chunks:
                    mm = three(out, whi[slot][:, k], wlo[slot][:, k], ah_, al_, start, stop)
                mm.then_inc(ty.sem("unit_used"), 1)

            def turned(out, rows, n, id_):
                if n == P:
                    return pe.transpose(out, rows, id_)
                return pe.matmul(out, rows, id_, start=True, stop=True)

            def sum_squares(tag, out, src):
                for k in range(DC):
                    pe.wait_ge(*at("squared", (tag, k)))
                    for o, s in zip(out, src(k)):
                        mm = pe.matmul(o, ones, s, start=k == 0, stop=k == DC - 1)
                    mm.then_inc(*tick("squares_summed", (tag, k)))

            pe.wait_ge(*at("const_in", 0))
            sum_squares("pre", [X[:, 0, :]], lambda k: [tmp[:, k % 2, 0:S]])
            for u in range(16):
                out = G[:, u % 2, :]
                if u >= 2:
                    pe.wait_ge(*at("evicted1", u - 2) if u % 2 == 0 else at("evicted1d", u - 2))
                if u == 0:
                    for k in range(DC):
                        pe.wait_ge(*at("h_low", ("pre", k)))
                if u in (U_VSL, U_VWN, U_VS):
                    pe.wait_ge(ty.sem("unit_split"), unit_ready(u))
                    for t in range(QT):
                        for k in range(DC):
                            mm = three(out[:, t * P:(t + 1) * P], whi[u % 2][:, k], wlo[u % 2][:, k],
                                       hh[:, k, t * P:(t + 1) * P], hl[:, k, t * P:(t + 1) * P],
                                       k == 0, k == DC - 1, flip=True)
                    mm.then_inc(ty.sem("unit_used"), 1)
                else:
                    unit(u, u % 2, out, [(k, out, hh[:, k, 0:S], hl[:, k, 0:S], k == 0, k == DC - 1)
                                         for k in range(DC)])
            pe.wait_ge(*at("wg_split", 1))
            for t in range(QT):
                for k in range(DC):
                    mm = three(X[:, 1, t * 24:(t + 1) * 24], wgh[:, k], wgl[:, k],
                               hh[:, k, t * P:(t + 1) * P], hl[:, k, t * P:(t + 1) * P],
                               k == 0, k == DC - 1, flip=True)
            mm.then_inc(*tick("gates_made", 0))

            for n in "kv":
                pe.wait_ge(*at(f"cw_in_{n}", 2))
                pe.wait_ge(*(at("evicted1", U_KC) if n == "k" else at("evicted1d", U_VC)))
                if n == "k":
                    pe.wait_ge(*at("vec_in", 0))
                ps = S0 if n == "k" else S1
                v0 = V_PEK if n == "k" else V_PEV
                for c in range(16):
                    pe.matmul(ps[:, 1, 0:1], cw1[n][:, c], vec[:, v0 + c:v0 + c + 1],
                              start=c == 0, stop=c == 15)
                for c in range(16):
                    mm = pe.matmul(ps[:, 0, 0:2 * NCMP], cw1[n][:, c],
                                   seg[n][:, :, 2 * c:2 * c + CMP_STRIDE * (NCMP - 1) + 1:CMP_STRIDE],
                                   start=c == 0, stop=c == 15)
                mm.then_inc(*tick("hidden_made", n))
            pe.wait_ge(*at("hidden", "k"))
            pe.matmul(S0[:, 1, 0:2 * NCMP], cw2["k"][:], hid["k"][:, 3, :], start=True, stop=True)\
                .then_inc(*tick("kcmp_made", 0))
            pe.wait_ge(*at("hidden", "v"))
            for g in range(GROUPS):
                mm = pe.matmul(S1[0:NCMP, 1, g * HD:(g + 1) * HD], hid["v"][:, 3, g * NCMP:(g + 1) * NCMP],
                               cw2["v"][:, 0:HD], start=True, stop=True)
            mm.then_inc(*tick("vcmp_made", 0))

            def score_bank(r):
                return (S0, S1)[r // 2][:, r % 2, :]

            def scores1(n):
                kind, g, t = jobs1[n]
                lo, nk = span1(kind, t)
                for r in range(REP):
                    h = g * REP + r
                    c, o = h // 2 + (4 if kind == "swa" else 0), (h % 2) * HD
                    keys = kcmp[o:o + HD, g, :] if kind == "cmp" else k1[kind][o:o + HD, g, lo:lo + nk]
                    if n:
                        pe.wait_ge(*at("biased", (n - 1, r)))
                    pe.matmul(score_bank(r)[:, 0:nk], q1[o:o + HD, c, t * P:(t + 1) * P], keys,
                              start=True, stop=True).then_inc(*tick("scored", (n, r)))

            for e in (at("evicted1", 14), at("evicted1d", 15), at("kcmp", 1), at("vcmp", 0)):
                pe.wait_ge(*e)
            turn = 0
            outs = 0
            scores1(0)
            for n, (kind, g, t) in enumerate(jobs1):
                if n + 1 < len(jobs1):
                    scores1(n + 1)
                for r in range(REP):
                    pe.wait_ge(*at("weighted", (n, r)))
                bl1 = blocks1(kind, t)
                for b, (k0, kn) in enumerate(bl1):
                    lo = span1(kind, t)[0]
                    bank = X[:, 0, :] if turn % 2 == 0 else G[:, 1, :]
                    if turn >= 2:
                        pe.wait_ge(*at("turned_out", turn - 2))
                    elif turn == 0:
                        pe.wait_ge(*at("rstd", "pre"))
                    for r in range(REP):
                        mm = turned(bank[0:kn, r * P:(r + 1) * P],
                                    probs[:, n % 2, r, k0 - lo:k0 - lo + kn], kn, ident)
                    mm.then_inc(*tick("turned", turn))
                    pe.wait_ge(*at("turned_out", turn))
                    if b == 0 and kind in ("cmp", "swa"):
                        if outs:
                            pe.wait_ge(*at("mix_low", outs - 1))
                        else:
                            pe.wait_ge(*at("gates", 0))
                    for half in range(2):
                        vals = vcmp[:, g, :] if kind == "cmp" else v1[kind][:, k0 // P, g * HD:(g + 1) * HD]
                        pr = pts[0:kn, turn % 2, :].rearrange("p (c a q) -> p c a q", c=2, a=2)[:, :, half, :]
                        mm = pe.matmul(X[half * HD:(half + 1) * HD, 1, 0:2 * P].rearrange("p (c q) -> p c q", c=2),
                                       vals, pr, start=b == 0 and kind in ("cmp", "swa"),
                                       stop=b == len(bl1) - 1 and last_of_output(kind))
                    mm.then_inc(*tick("weighed", turn))
                    turn += 1
                if last_of_output(kind):
                    outs += 1

            pe.wait_ge(*at("mix_low", outs - 1))
            for m in range(DC):
                u = U_WO + m
                if m >= 2:
                    pe.wait_ge(*at("mixed", m - 2))
                unit(u, u % 2, None, [(k, G[:, m % 2, :], hh[:, k, 0:S], hl[:, k, 0:S], k == 0, k == DC - 1)
                                      for k in range(DC)])
            sum_squares("post", [X[:, 0, :]], lambda k: [tmp[:, k % 2, 0:S]])
            sum_squares("mpre", [X[:, 1, :]], lambda k: [tmp[:, k % 2, 0:S]])

            pe.wait_ge(*at("h_low", ("mpre", DC - 1)))

            def gate_up(i, first):
                for pair in range(2):
                    if not first:
                        pe.wait_ge(ty.sem("act_low"), 2 * i + pair - 1)
                    for j in range(2):
                        pe.wait_ge(ty.sem("unit_split"), 4 * i + (U_GU + 2 * pair + j + 1))
                        for k in range(DC):
                            mm = three((G, S0)[pair][:, j, :], whi[j][:, k], wlo[j][:, k],
                                       hh[:, k, 0:S], hl[:, k, 0:S], k == 0, k == DC - 1)
                        mm.then_inc(ty.sem("unit_used"), 1)

            gate_up(0, True)
            with pe.Fori(1, FC // 2) as i:
                gate_up(i, False)

            pe.wait_ge(ty.sem("act_low"), FC)
            for m in range(DC):
                for k in range(FC):
                    tile = m * FC + k
                    u = U_DOWN + tile // 8
                    if tile % 8 == 0:
                        pe.wait_ge(ty.sem("unit_split"), unit_ready(u))
                    if k == 0 and m >= 2:
                        pe.wait_ge(*at("downed", m - 2))
                    mm = three(G[:, m % 2, :], whi[u % 2][:, tile % 8], wlo[u % 2][:, tile % 8],
                               acth[:, k, :], actl[:, k, :], k == 0, k == FC - 1)
                    if tile % 8 == 7:
                        mm.then_inc(ty.sem("unit_used"), 1)
            sum_squares("mpost", [X[:, 0, :]], lambda k: [tmp[:, k % 2, 0:S]])

            pe.wait_ge(*at("x_low", DC - 1))
            pe.wait_ge(*at("p_low", 0))
            for m in range(DC):
                for k in range(DC + PLE_C):
                    tile = m * (DC + PLE_C) + k
                    u = U_PLE + tile // 8
                    if tile % 8 == 0:
                        pe.wait_ge(ty.sem("unit_split"), unit_ready(u))
                    if k == 0 and m >= 2:
                        pe.wait_ge(*at("x_new", ("ple", m - 2)))
                    gate = k < DC
                    out = (G, S0)[m % 2][:, 0 if gate else 1, :]
                    mm = three(out, whi[u % 2][:, tile % 8], wlo[u % 2][:, tile % 8],
                               hh[:, k, 0:S] if gate else ph[:, k - DC, :],
                               hl[:, k, 0:S] if gate else pl[:, k - DC, :],
                               k in (0, DC), k in (DC - 1, DC + PLE_C - 1))
                    if tile % 8 == 7:
                        mm.then_inc(ty.sem("unit_used"), 1)

            with pe.Fori(0, LAYERS) as l:
                ty.enter("layer", l, LAYERS)

                def lunit(m, g_wait, outs, chunks):
                    if g_wait:
                        pe.wait_ge(*g_wait)
                    pe.wait_ge(ty.sem("unit_split"), l * L_UNITS + (U_LAYER + m + 1))
                    for k, out, a, b, start, stop in chunks:
                        for tok in range(2):
                            cols = slice(tok * TH, (tok + 1) * TH)
                            mm = three(out[:, tok, 0:TH], whi[m % 2][:, k], wlo[m % 2][:, k],
                                       a[:, cols], b[:, cols], start, stop)
                    mm.then_inc(ty.sem("unit_used"), 1)

                def project(m, g_wait):
                    lunit(m, g_wait, G, [(k, G, hh[:, k, :], hl[:, k, :], k == 0, k == DC - 1)
                                         for k in range(DC)])

                def plain(out, lhs, rhs):
                    for tok in range(2):
                        mm = pe.matmul(out[:, tok, 0:TH], lhs, rhs[:, tok * TH:(tok + 1) * TH],
                                       start=True, stop=True)
                    return mm

                sum_squares("layer", [X[:, 0, 0:TH], X[:, 1, 0:TH]],
                            lambda k: [probs2[:, k % 2, 0:TH], probs2[:, k % 2, TH:T]])
                for k in range(DC):
                    pe.wait_ge(*at("h_low", ("layer", k)))
                project(L_K, None)
                pe.wait_ge(*at("k_raw", 0))
                plain(X, bones, probs2[:, 0, :]).then_inc(*tick("k_squares", 0))
                plain(S0, rot, probs2[:, 1, :]).then_inc(*tick("k_turned", 0))
                pe.wait_ge(ty.sem("unit_split"), l * L_UNITS + (U_LAYER + L_V + 1))
                for j in range(QT + 1):
                    t0 = rows2(j)[0]
                    for k in range(DC):
                        mm = three(G[:, 0, j * 72:(j + 1) * 72], whi[1][:, k, 0:72], wlo[1][:, k, 0:72],
                                   hh[:, k, t0:t0 + P], hl[:, k, t0:t0 + P], k == 0, k == DC - 1, flip=True)
                mm.then_inc(ty.sem("unit_used"), 1)
                for c in range(8):
                    isq = c >= 4
                    project(L_QI + c, at("v_out", 0) if c == 0 else at("q_raw", c - 1))
                    pe.wait_ge(*at("q_raw", c))
                    if c == 0:
                        pe.wait_ge(*at("k_ready", 0))
                    if c >= 2:
                        pe.wait_ge(*at("q_ready", c - 2))
                    buf = (qi2, q2)[isq][:, c % 4, :]
                    plain((S0, S1)[c % 2], rot, buf).then_inc(*tick("q_turned", c))
                    if isq:
                        for j in range(QT + 1):
                            t0, m = rows2(j)
                            mm = pe.matmul(X[0:m, 0, j * 8 + 2 * (c - 4):j * 8 + 2 * (c - 4) + 2],
                                           probs2[:, c % 2, t0:t0 + m], bones[:, 0:P:HD],
                                           start=True, stop=True)
                        mm.then_inc(*tick("q_squares", c))
                for c in range(6, 8):
                    pe.wait_ge(*at("q_ready", c))

                readers = []
                turn = 0

                def take_scores(reader):
                    if len(readers) >= 2:
                        pe.wait_ge(*at(*readers[-2]))
                        hold(pe)
                    readers.append(reader)
                    return (S0, S1)[(len(readers) - 1) % 2]

                g_last = at("q_raw", 7)

                for j in range(QT + 1):
                    t0, m = rows2(j)
                    n = seen2(j)
                    if j:
                        for h in range(HEADS):
                            o = (h % 2) * HD
                            ps = take_scores(("relued", (j, h)))
                            for a, w in parts2(n):
                                mm = pe.matmul(ps[0:m, a // TH if n > 512 else 0, 0:w],
                                               qi2[o:o + HD, h // 2, t0:t0 + m], kiT2[o:o + HD, a:a + w],
                                               start=True, stop=True)
                            mm.then_inc(*tick("index_scored", (j, h)))
                    for kind, c in filler[j]:
                        project(unit_of(kind, c), g_last)
                        g_last = at("g_read_d" if kind in ("gb", "ga") else "g_read_a", (kind, c))
                        if kind == "ub":
                            pe.wait_ge(*at("pooled", c))
                            if c == 0:
                                pe.wait_ge(*at("poolw_in", 0))
                            plain(G, poolw[:, c, :], pooled(c)).then_inc(*tick("pool_mixed", c))
                            g_last = at("g_read_d", ("pm", c))
                    for half in range(2):
                        for r in range(REP):
                            h = half * REP + r
                            o = (h % 2) * HD
                            ps = take_scores(("masked", (j, half, r)))
                            for a, w in parts2(n):
                                mm = pe.matmul(ps[0:m, a // TH if n > 512 else 0, 0:w],
                                               q2[o:o + HD, h // 2, t0:t0 + m], kT2[o:o + HD, a:a + w],
                                               start=True, stop=True)
                            mm.then_inc(*tick("scored2", (j, half, r)))
                        for r in range(REP):
                            pe.wait_ge(*at("weighted2", (j, half, r)))
                        for b in range(j + 1):
                            k0, kn = rows2(b)
                            pe.wait_ge(*(at("turned_out2", turn - 1) if turn else at("rq", 0)))
                            hold(pe)
                            for r in range(REP):
                                mm = turned(X[0:kn, 0, r * m:(r + 1) * m], probs2[0:m, r, k0:k0 + kn], kn,
                                            ident[0:m, 0:m])
                            mm.then_inc(*tick("turned2", turn))
                            if b == 0 and (j or half):
                                pe.wait_ge(*at("a_low", (j, half - 1) if half else (j - 1, 1)))
                            pe.wait_ge(*at("turned_out2", turn))
                            hold(pe)
                            for odd in range(2):
                                pr = pts[0:kn, turn % 2, 0:REP * m].rearrange("p (c a q) -> p c a q", c=2, a=2)
                                mm = pe.matmul(X[odd * HD:(odd + 1) * HD, 1, 0:2 * m]
                                               .rearrange("p (c q) -> p c q", c=2),
                                               v2[0:kn, b, 0:HD], pr[:, :, odd, :],
                                               start=b == 0, stop=b == j)
                            mm.then_inc(*tick("weighed2", turn))
                            turn += 1

                pe.wait_ge(*g_last)
                pe.wait_ge(*at("a_low", (QT, 1)))
                pe.wait_ge(*at("b_low", POOL_C - 1))
                for m in range(DC):
                    pair = (G, S0) if m % 2 == 0 else (S1, X)
                    if m >= 2:
                        pe.wait_ge(*at("z_low", m - 2))
                    lunit(L_WAB + m, None, None,
                          [(k, pair[0], ah[:, k, :], al[:, k, :], k == 0, k == 3) for k in range(4)] +
                          [(k + 4, pair[1], bh[:, k, :], bl[:, k, :], k == 0, k == 3) for k in range(4)])
                for k in range(DC - 2, DC):
                    pe.wait_ge(*at("z_low", k))
                for m in range(DC):
                    out = (G, S0)[m % 2]
                    lunit(L_OUT + m, at("x_new", ("layer", m - 2)) if m >= 2 else None, None,
                          [(k, out, hh[:, k, :], hl[:, k, :], k == 0, k == DC - 1) for k in range(DC)])
                ty.leave()

        @block.scalar
        def _(act):
            def square_all(tag, src, ready, squares, layer=None):
                for k in range(DC):
                    sem, value = ready(k)
                    act.wait_ge(sem, value if layer is None else layer * DC + value)
                    if k >= 2:
                        act.wait_ge(*at("squares_summed", (tag, k - 2)))
                    act.activation(squares(k), src(k), ACT.Square).then_inc(*tick("squared", (tag, k)))

            def root(tag, out, summed, scale):
                act.wait_ge(*at("squares_summed", (tag, DC - 1)))
                act.activation(out, summed, ACT.Sqrt, bias=eps, scale=scale).then_inc(*tick("rms", tag))

            def high_parts(tag, src, out):
                for k in range(DC):
                    act.wait_ge(*at("normed", (tag, k)))
                    act.activation(out(k), src(k), ACT.Copy).then_inc(*tick("h_high", (tag, k)))

            act.wait_ge(*at("const_in", 0))
            square_all("pre", lambda k: x[:, k, META:T], lambda k: at("x_in", 0), lambda k: tmp[:, k % 2, 0:S])
            root("pre", rstd[:, 0:S], X[:, 0, :], 1.0 / D)
            high_parts("pre", lambda k: tmp[:, 2 + k % 2, 0:S], lambda k: hh[:, k, 0:S])
            for u in range(0, 16, 2):
                act.wait_ge(ty.sem("unit_used"), unit_ready(u))
                ps = G[:, 0, :]
                if u == U_KC:
                    act.copy(seg["k"][0:HD, 0, :], ps[0:HD, :])
                    act.copy(seg["k"][0:HD, 1, :], ps[HD:P, :])
                    act.copy(seg["k"][HD:P, 0, 0:S - 1], ps[0:HD, 1:S])
                    ins = act.copy(seg["k"][HD:P, 1, 0:S - 1], ps[HD:P, 1:S])
                elif u in (U_KSL, U_KS):
                    dst = k1["slc" if u == U_KSL else "swa"]
                    for g in range(GROUPS):
                        act.copy(dst[0:HD, g, :], ps[g * HD:(g + 1) * HD, :])
                        ins = act.copy(dst[HD:P, g, :], ps[g * HD:(g + 1) * HD, :])
                elif u == U_VWN:
                    ins = act.copy(v1["win"][:, :, :], ps.rearrange("p (t c) -> p t c", t=QT))
                else:
                    ins = act.copy(q1[:, u - U_Q, :], ps)
                ins.then_inc(*tick("evicted1", u))
            act.wait_ge(*at("gates_made", 0))
            act.activation(gates[:, 0], X[:, 1, 0:QT * 24].rearrange("p (t c) -> p t c", t=QT), ACT.Tanh,
                           scale=0.5).then_inc(*tick("gates_tanh", 0))

            for n in "kv":
                act.wait_ge(*at("gelu_in", n))
                act.activation(hid[n][:, 2], hid[n][:, 1], ACT.Tanh, scale=GELU_A)\
                    .then_inc(*tick("gelu_tanh", n))
            act.wait_ge(*at("kcmp_made", 0))
            for half in range(2):
                ins = act.copy(kcmp[half * HD:(half + 1) * HD, :, :],
                               S0[half * HD:(half + 1) * HD, 1, 0:2 * NCMP].rearrange("p (g n) -> p g n", g=2))
                ins.then_inc(*tick("kcmp", half))
            act.wait_ge(*at("vcmp_made", 0))
            act.copy(vcmp[:, :, :], S1[0:NCMP, 1, 0:2 * HD].rearrange("p (g n) -> p g n", g=2))\
                .then_inc(*tick("vcmp", 0))

            turn = 0
            outs = 0

            def turned_out(n):
                nonlocal turn, outs
                kind, g, t = jobs1[n]
                for k0, kn in blocks1(kind, t):
                    act.wait_ge(*at("turned", turn))
                    if turn >= 2:
                        act.wait_ge(*at("weighed", turn - 2))
                    bank = X[:, 0, :] if turn % 2 == 0 else G[:, 1, :]
                    act.copy(pts[0:kn, turn % 2, :], bank[0:kn, :]).then_inc(*tick("turned_out", turn))
                    turn += 1
                if last_of_output(kind):
                    act.wait_ge(*at("weighed", turn - 1))
                    c = 2 * g + (4 if kind == "swa" else 0)
                    act.copy(hh[:, c:c + 2, t * P:(t + 1) * P],
                             X[:, 1, 0:2 * P].rearrange("p (c q) -> p c q", c=2)).then_inc(*tick("mix_high", outs))
                    outs += 1

            for n, (kind, g, t) in enumerate(jobs1):
                nk = span1(kind, t)[1]
                act.wait_ge(*at("neg_max", n))
                for r in range(REP):
                    pr = probs[:, n % 2, r, 0:nk]
                    act.activation(pr, pr, ACT.Exp, bias=small[:, 8 * (n % 2) + 1, r:r + 1], scale=SCALE,
                                   accum_out=small[:, 8 * (n % 2) + 2, r:r + 1]).then_inc(*tick("exped", (n, r)))
                if kind == "swa":
                    act.activation(small[:, 8 * (n % 2) + 4, 0:REP], small[:, 8 * (n % 2) + 3, 0:REP], ACT.Exp)\
                        .then_inc(*tick("sink_exp", n))
                if n:
                    turned_out(n - 1)
            turned_out(len(jobs1) - 1)

            def y(m):
                return probs[:, m // 4, m % 4, 0:S]

            for m in range(DC):
                act.wait_ge(ty.sem("unit_used"), unit_ready(U_WO + m))
                act.copy(y(m), G[:, m % 2, :]).then_inc(*tick("mixed", m))
            square_all("post", y, lambda k: at("mixed", k), lambda k: tmp[:, k % 2, 0:S])
            root("post", rstd[:, 0:S], X[:, 0, :], 1.0 / D)
            square_all("mpre", lambda k: x[:, k, META:T], lambda k: at("x_new", ("post", k)),
                       lambda k: tmp[:, k % 2, 0:S])
            root("mpre", rstd[:, 0:S], X[:, 1, :], 1.0 / D)
            high_parts("mpre", lambda k: tmp[:, 2 + k % 2, 0:S], lambda k: hh[:, k, 0:S])

            def gate_up(i):
                for pair in range(2):
                    n = 2 * i + pair
                    act.wait_ge(ty.sem("conv_done"), n + 1)
                    act.activation(probs[:, pair, 1, 0:S], probs[:, pair, 0, 0:S], ACT.Square)\
                        .then_inc(ty.sem("conv_squared"), 1)
                    act.wait_ge(ty.sem("act_in"), n + 1)
                    act.activation(probs[:, pair, 1, 0:S], probs[:, pair, 2, 0:S], ACT.Tanh, scale=GELU_A)\
                        .then_inc(ty.sem("act_tanh"), 1)
                    act.wait_ge(ty.sem("act_full"), n + 1)
                    act.activation(acth[:, n, :], probs[:, pair, 3, 0:S], ACT.Copy)\
                        .then_inc(ty.sem("act_high"), 1)

            with act.Fori(0, FC // 2) as i:
                gate_up(i)

            for m in range(DC):
                u = U_DOWN + ((m + 1) * FC - 1) // 8
                act.wait_ge(ty.sem("unit_used"), unit_ready(u))
                act.copy(y(m), G[:, m % 2, :]).then_inc(*tick("downed", m))
            act.dma_start(pT[:], io["p"]).then_inc(*tick("p_in", 0, 16))
            square_all("mpost", y, lambda k: at("downed", k), lambda k: tmp[:, k % 2, 0:S])
            root("mpost", rstd[:, 0:S], X[:, 0, :], 1.0 / D)
            act.wait_ge(*at("p_in", 0))
            act.copy(ph[:], pT[:]).then_inc(*tick("p_high", 0))
            for k in range(DC):
                act.wait_ge(*at("x_new", ("mpost", k)))
                act.copy(hh[:, k, 0:S], x[:, k, META:T]).then_inc(*tick("x_high", k))
            for m in range(DC):
                u = U_PLE + ((m + 1) * (DC + PLE_C) - 1) // 8
                act.wait_ge(ty.sem("unit_used"), unit_ready(u))
                if m >= 2:
                    act.wait_ge(*at("x_new", ("ple", m - 2)))
                act.activation(tmp[:, m % 2, 0:S], (G, S0)[m % 2][:, 0, :], ACT.Tanh, scale=0.5)\
                    .then_inc(*tick("ple_tanh", m))

            with act.Fori(0, LAYERS) as l:
                ty.enter("layer", l, LAYERS)

                def unit_wait(m):
                    act.wait_ge(ty.sem("unit_used"), l * L_UNITS + (U_LAYER + m + 1))

                sem, value = at("x_new", ("ple", DC - 1))
                act.wait_ge(sem, l * DC + value)
                act.dma_start(lvec[:], io["lvec"][l]).then_inc(*tick("lvec_in", 0, 16))
                act.dma_start(poolw[:], io["poolw"][l]).then_inc(*tick("poolw_in", 0, 16))
                act.wait_ge(*at("meta_in", 0))
                square_all("layer", lambda k: x[:, k, :], lambda k: at("x_new", ("ple", k)),
                           lambda k: probs2[:, k % 2, :], layer=l)
                root("layer", halves(score[:, 0, :]), full(X), 1.0 / D)
                high_parts("layer", lambda k: probs2[:, 2 + k % 2, :], lambda k: hh[:, k, :])

                unit_wait(L_K)
                act.wait_ge(*at("lvec_in", 0))
                act.activation(halves(probs2[:, 0, :]), full(G), ACT.Square)
                act.activation(halves(probs2[:, 1, :]), full(G), ACT.Copy, scale=lvec[:, W_KN:W_KN + 1])\
                    .then_inc(*tick("k_raw", 0))
                act.wait_ge(*at("k_squares", 0))
                act.activation(halves(score[:, 0, :]), full(X), ACT.Sqrt, bias=eps, scale=1.0 / HD)\
                    .then_inc(*tick("k_rms", 0))
                unit_wait(L_V)
                made = G[:, 0, 0:(QT + 1) * 72].rearrange("p (j c) -> p j c", j=QT + 1)
                act.copy(v2[:, :, 0:HD], made[:, :, 0:HD])
                act.activation(v2[:, :, HD:72], made[:, :, HD:72], ACT.Copy, scale=(8 ** -0.5) * (HD ** -0.5))\
                    .then_inc(*tick("v_out", 0))
                for c in range(8):
                    unit_wait(L_QI + c)
                    if c < 4:
                        act.copy(halves(qi2[:, c, :]), full(G)).then_inc(*tick("q_raw", c))
                    else:
                        if c == 4:
                            act.wait_ge(*at("k_ready", 1))
                        if c >= 6:
                            act.wait_ge(*at("q_squares", c - 2))
                        act.activation(halves(probs2[:, c % 2, :]), full(G), ACT.Square)
                        act.activation(halves(q2[:, c - 4, :]), full(G), ACT.Copy,
                                       scale=lvec[:, W_QN:W_QN + 1]).then_inc(*tick("q_raw", c))
                act.wait_ge(*at("q_squares", 7))
                act.activation(rq[0:META, 0, 0, :], X[0:META, 0, 0:8], ACT.Sqrt, bias=const[0:META, C_EPS:C_EPS + 1],
                               scale=1.0 / HD)
                act.activation(rq[:, 0, 1:, :], X[:, 0, 8:40].rearrange("p (j h) -> p j h", h=8), ACT.Sqrt,
                               bias=eps, scale=1.0 / HD).then_inc(*tick("rq_rms", 0))

                turn = 0
                for j in range(QT + 1):
                    t0, m = rows2(j)
                    n = seen2(j)
                    if j:
                        for h in range(HEADS):
                            act.wait_ge(*at("index_scored", (j, h)))
                            if h >= 2:
                                act.wait_ge(*at("indexed", (j, h - 2)))
                            elif h == 0:
                                act.wait_ge(*at("a_low", (j - 1, 1)))
                            ps = (S0, S1)[bank_of[("relued", (j, h))]]
                            act.activation(wide(relu[0:m, h % 2, 0:n], n), scores2(ps, m, n), ACT.Relu)\
                                .then_inc(*tick("relued", (j, h)))
                    for kind, c in filler[j]:
                        unit_wait(unit_of(kind, c))
                        if kind == "gb":
                            if c:
                                act.wait_ge(*at("branch_b", c - 1))
                            act.activation(halves(gateb), full(G), ACT.Tanh, scale=0.5)\
                                .then_inc(*tick("gateb_tanh", c))
                        elif kind == "ub":
                            if c:
                                act.wait_ge(*at("b_low", c - 1))
                            act.copy(halves(pool3[:, 0, META:META + T]), full(G))\
                                .then_inc(*tick("g_read_a", (kind, c)))
                            act.wait_ge(*at("branch_b", c))
                            act.copy(bh[:, c, :], pool3[:, 1, META:META + T]).then_inc(*tick("b_high", c))
                        elif kind == "ga":
                            act.activation(halves(sila[:, c, :]), full(G), ACT.Tanh, scale=0.5)\
                                .then_inc(*tick("gatea_tanh", c))
                        else:
                            if c == 11:
                                act.wait_ge(*at("b_low", POOL_C - 1))
                            act.activation(halves(merge[:, c, :]), full(G), ACT.Tanh, scale=0.5)\
                                .then_inc(*tick("g_read_a", (kind, c)))
                    for half in range(2):
                        act.wait_ge(*at("neg_max2", (j, half)))
                        for r in range(REP):
                            pr = probs2[0:m, r, 0:n]
                            act.activation(pr, pr, ACT.Exp, bias=small[0:m, 1, r:r + 1],
                                           scale=rq[0:m, 2, j, half * REP + r:half * REP + r + 1],
                                           accum_out=small[0:m, 2, r:r + 1]).then_inc(*tick("exped2", (j, half, r)))
                        for b in range(j + 1):
                            kn = rows2(b)[1]
                            act.wait_ge(*at("turned2", turn))
                            if turn >= 2:
                                act.wait_ge(*at("weighed2", turn - 2))
                            act.copy(pts[0:kn, turn % 2, 0:REP * m], X[0:kn, 0, 0:REP * m])\
                                .then_inc(*tick("turned_out2", turn))
                            turn += 1
                        act.wait_ge(*at("gated_a", (j, half)))
                        act.copy(ah[:, 2 * half:2 * half + 2, t0:t0 + m],
                                 relu[:, 0:2, 0:m]).then_inc(*tick("a_high", (j, half)))

                for k in range(DC):
                    act.wait_ge(*at("merged", k))
                    act.activation(hh[:, k, :], merge[:, k, :], ACT.Copy, scale=0.5)\
                        .then_inc(*tick("z_high", k))
                ty.leave()

        @block.vector
        def _(dve):
            def norm(tag, src, normed, cols, gain, r, out=None):
                dve.wait_ge(*at("rms", tag))
                dve.reciprocal(r, r).then_inc(*tick("rstd", tag))
                dve.wait_ge(*at("rstd", tag))

                def low(k):
                    dve.wait_ge(*at("h_high", (tag, k)))
                    dve.tensor_tensor(out[1](k), normed(k), out[0](k).bitcast(F32), ALU.subtract)\
                        .then_inc(*tick("h_low", (tag, k)))

                for k in range(DC):
                    if out and k >= 2:
                        dve.wait_ge(*at("h_low", (tag, k - 2)))
                    elif k >= 2:
                        dve.wait_ge(*at("x_new", (tag, k - 2)))
                    dve.scalar_tensor_tensor(out=normed(k), in0=src(k), scalar=gain(k), in1=r,
                                             op0=ALU.mult, op1=ALU.mult).then_inc(*tick("normed", (tag, k)))
                    if out:
                        if k:
                            low(k - 1)
                    else:
                        dve.wait_ge(*at("normed", (tag, k)))
                        xs = x[:, k, cols]
                        dve.tensor_tensor(xs, xs, normed(k), ALU.add).then_inc(*tick("x_new", (tag, k)))
                if out:
                    low(DC - 1)

            def vcol(v0):
                return lambda k: vec[:, v0 + k:v0 + k + 1]

            seq = slice(META, T)
            dve.wait_ge(*at("vec_in", 0))
            norm("pre", lambda k: x[:, k, seq], lambda k: tmp[:, 2 + k % 2, 0:S], seq, vcol(V_PRE),
                 rstd[:, 0:S], (lambda k: hh[:, k, 0:S], lambda k: hl[:, k, 0:S]))
            dve.wait_ge(*at("wg_in", 0))
            dve.tensor_copy(wgh[:], wg[:]).then_inc(*tick("wg_split", 0))
            dve.wait_ge(*at("wg_split", 0))
            dve.tensor_tensor(wgl[:], wg[:], wgh[:].bitcast(F32), ALU.subtract).then_inc(*tick("wg_split", 1))
            for h in range(HEADS):
                dve.tensor_scalar(bias1[:, h, :], const[:, C_DIST:C_DIST + S], -slope(HEADS + h) / SCALE, None,
                                  ALU.mult).then_inc(*tick("bias1", h))
            for u in range(1, 16, 2):
                dve.wait_ge(ty.sem("unit_used"), unit_ready(u))
                ps = G[:, 1, :]
                if u == U_VC:
                    dve.tensor_copy(seg["v"][0:HD, 0, :], ps[0:HD, :])
                    dve.tensor_copy(seg["v"][0:HD, 1, :], ps[HD:P, :])
                    dve.tensor_copy(seg["v"][HD:P, 0, 0:S - 1], ps[0:HD, 1:S])
                    ins = dve.tensor_copy(seg["v"][HD:P, 1, 0:S - 1], ps[HD:P, 1:S])
                elif u == U_KWN:
                    for g in range(GROUPS):
                        dve.tensor_copy(k1["win"][0:HD, g, :], ps[g * HD:(g + 1) * HD, :])
                        ins = dve.tensor_copy(k1["win"][HD:P, g, :], ps[g * HD:(g + 1) * HD, :])
                elif u in (U_VSL, U_VS):
                    ins = dve.tensor_copy(v1["slc" if u == U_VSL else "swa"][:, :, :],
                                          ps.rearrange("p (t c) -> p t c", t=QT))
                else:
                    ins = dve.tensor_copy(q1[:, u - U_Q, :], ps)
                ins.then_inc(*tick("evicted1d", u))
            dve.wait_ge(*at("gates_tanh", 0))
            dve.tensor_scalar(gates[:, 1], gates[:, 0], 1.0, 0.5, ALU.add, ALU.mult)\
                .then_inc(*tick("gates_half", 0))
            dve.wait_ge(*at("gates_half", 0))
            for t in range(QT):
                ins = dve.tensor_scalar(gates[:, 2, t, :], gates[:, 1, t, :], const[:, C_SOME + t:C_SOME + t + 1],
                                        None, ALU.mult)
            ins.then_inc(*tick("gates", 0))

            for n in "kv":
                i = "kv".index(n)
                ps = S0 if n == "k" else S1
                a = hid[n]
                dve.wait_ge(*at("hidden_made", n))
                dve.tensor_copy(pecol[:, i:i + 1], ps[:, 1, 0:1]).then_inc(*tick("pe_col", n))
                dve.wait_ge(*at("pe_col", n))
                dve.tensor_scalar(a[:, 0], ps[:, 0, 0:2 * NCMP], pecol[:, i:i + 1], None, ALU.add)\
                    .then_inc(*tick("hid_step", (n, 0)))
                dve.wait_ge(*at("hid_step", (n, 0)))
                dve.tensor_tensor(a[:, 1], a[:, 0], a[:, 0], ALU.mult).then_inc(*tick("hid_step", (n, 1)))
                dve.wait_ge(*at("hid_step", (n, 1)))
                dve.tensor_scalar(a[:, 3], a[:, 1], GELU_B, 1.0, ALU.mult, ALU.add)\
                    .then_inc(*tick("hid_step", (n, 2)))
                dve.wait_ge(*at("hid_step", (n, 2)))
                dve.tensor_tensor(a[:, 1], a[:, 3], a[:, 0], ALU.mult).then_inc(*tick("gelu_in", n))
                dve.wait_ge(*at("gelu_tanh", n))
                dve.tensor_scalar(a[:, 1], a[:, 2], 1.0, 0.5, ALU.add, ALU.mult)\
                    .then_inc(*tick("hid_step", (n, 3)))
                dve.wait_ge(*at("hid_step", (n, 3)))
                dve.tensor_tensor(a[:, 3], a[:, 1], a[:, 0], ALU.mult).then_inc(*tick("hidden", n))

            def biased(n):
                kind, g, t = jobs1[n]
                lo, nk = span1(kind, t)
                st = small[:, 8 * (n % 2):8 * (n % 2) + 8, :]
                if n >= 2:
                    dve.wait_ge(*at("weighed", last_turn[n - 2]))
                for r in range(REP):
                    h = g * REP + r
                    dve.wait_ge(*at("scored", (n, r)))
                    ps = (S0, S1)[r // 2][:, r % 2, 0:nk]
                    pr = probs[:, n % 2, r, 0:nk]
                    if kind in ("slc", "win"):
                        dve.wait_ge(*at("bias1", h))
                        d0 = 384 - t * P
                        dve.tensor_tensor_reduce(pr, ps, bias1[:, h, d0:d0 + nk], 1.0, -3e38, ALU.add, ALU.max,
                                                 st[:, 0, r:r + 1]).then_inc(*tick("biased", (n, r)))
                    else:
                        if kind == "cmp":
                            table = const[:, C_CDIST + 32 * t:C_CDIST + 32 * t + NCMP]
                            sl = slope(HEADS + h)
                        else:
                            table = const[:, C_SDIST + 2 * P - nk:C_SDIST + 2 * P]
                            sl = slope(h)
                        dve.scalar_tensor_tensor(out=pr, in0=table, scalar=-sl / SCALE, in1=ps, op0=ALU.mult,
                                                 op1=ALU.add).then_inc(*tick("biased", (n, r)))
                if kind not in ("slc", "win"):
                    dve.wait_ge(*at("biased", (n, REP - 1)))
                    dve.tensor_reduce(st[:, 0, 0:REP], probs[:, n % 2, :, 0:nk], mybir.AxisListType.X, ALU.max)\
                        .then_inc(*tick("row_max", n))
                    dve.wait_ge(*at("row_max", n))
                else:
                    dve.wait_ge(*at("biased", (n, REP - 1)))
                if kind != "swa":
                    dve.tensor_scalar(st[:, 1, 0:REP], st[:, 0, 0:REP], -SCALE, None, ALU.mult)\
                        .then_inc(*tick("neg_max", n))
                else:
                    sink = vec[:, V_SINK + g * REP:V_SINK + (g + 1) * REP]
                    dve.scalar_tensor_tensor(out=st[:, 5, 0:REP], in0=st[:, 0, 0:REP], scalar=SCALE, in1=sink,
                                             op0=ALU.mult, op1=ALU.max).then_inc(*tick("sink_step", (n, 0)))
                    dve.wait_ge(*at("sink_step", (n, 0)))
                    dve.tensor_tensor(st[:, 3, 0:REP], sink, st[:, 5, 0:REP], ALU.subtract)
                    dve.tensor_scalar(st[:, 1, 0:REP], st[:, 5, 0:REP], -1.0, None, ALU.mult)\
                        .then_inc(*tick("neg_max", n))

            def weighted(n):
                kind, g, t = jobs1[n]
                nk = span1(kind, t)[1]
                st = small[:, 8 * (n % 2):8 * (n % 2) + 8, :]
                dve.wait_ge(*at("exped", (n, REP - 1)))
                total = st[:, 2, 0:REP]
                if kind == "swa":
                    dve.wait_ge(*at("sink_exp", n))
                    dve.tensor_tensor(st[:, 6, 0:REP], total, st[:, 4, 0:REP], ALU.add)\
                        .then_inc(*tick("sum_step", (n, 0)))
                    dve.wait_ge(*at("sum_step", (n, 0)))
                    total = st[:, 6, 0:REP]
                dve.reciprocal(st[:, 7, 0:REP], total).then_inc(*tick("sum_step", (n, 1)))
                dve.wait_ge(*at("sum_step", (n, 1)))
                factor = st[:, 7, :]
                if kind != "swa":
                    b = ("cmp", "slc", "win").index(kind)
                    gate = gates[:, 2 if kind == "cmp" else 1, t, 12 * g + b:12 * g + b + 10:3]
                    dve.tensor_tensor(st[:, 6, 0:REP], st[:, 7, 0:REP], gate, ALU.mult)\
                        .then_inc(*tick("sum_step", (n, 2)))
                    dve.wait_ge(*at("sum_step", (n, 2)))
                    factor = st[:, 6, :]
                for r in range(REP):
                    pr = probs[:, n % 2, r, 0:nk]
                    dve.tensor_scalar(pr, pr, factor[:, r:r + 1], None, ALU.mult)\
                        .then_inc(*tick("weighted", (n, r)))

            last_turn = []
            for kind, g, t in jobs1:
                last_turn.append((last_turn[-1] if last_turn else -1) + len(blocks1(kind, t)))
            outs = 0
            biased(0)
            for n, (kind, g, t) in enumerate(jobs1):
                if n + 1 < len(jobs1):
                    biased(n + 1)
                weighted(n)
                if last_of_output(kind):
                    dve.wait_ge(*at("mix_high", outs))
                    c = 2 * g + (4 if kind == "swa" else 0)
                    sel = (slice(None), slice(c, c + 2), slice(t * P, (t + 1) * P))
                    dve.tensor_tensor(hl[sel], X[:, 1, 0:2 * P].rearrange("p (c q) -> p c q", c=2),
                                      hh[sel].bitcast(F32), ALU.subtract).then_inc(*tick("mix_low", outs))
                    outs += 1

            def y(m):
                return probs[:, m // 4, m % 4, 0:S]

            norm("post", y, lambda k: tmp[:, 2 + k % 2, 0:S], seq, vcol(V_POST), rstd[:, 0:S])
            norm("mpre", lambda k: x[:, k, seq], lambda k: tmp[:, 2 + k % 2, 0:S], seq, vcol(V_MPRE),
                 rstd[:, 0:S], (lambda k: hh[:, k, 0:S], lambda k: hl[:, k, 0:S]))

            def gate_up(i):
                for pair in range(2):
                    n = 2 * i + pair
                    ps = (G, S0)[pair]
                    conv, work, inner, full_ = (probs[:, pair, s, 0:S] for s in range(4))

                    def step(ins, k):
                        ins.then_inc(ty.sem("conv_step"), 1)
                        dve.wait_ge(ty.sem("conv_step"), 4 * n + k)

                    def cw(k):
                        return vec[:, V_CONVW + k * FC:V_CONVW + (k + 1) * FC][:, bass.ds(n, 1)]

                    dve.wait_ge(ty.sem("unit_used"), 4 * i + (U_GU + 2 * pair + 2))
                    step(dve.tensor_scalar(conv, ps[:, 0, :], cw(2), vec[:, V_CONVB:V_CONVB + FC][:, bass.ds(n, 1)],
                                           ALU.mult, ALU.add), 1)
                    step(dve.scalar_tensor_tensor(out=conv[:, 1:S], in0=ps[:, 0, 0:S - 1], scalar=cw(1),
                                                  in1=conv[:, 1:S], op0=ALU.mult, op1=ALU.add), 2)
                    dve.scalar_tensor_tensor(out=conv[:, 2:S], in0=ps[:, 0, 0:S - 2], scalar=cw(0),
                                             in1=conv[:, 2:S], op0=ALU.mult, op1=ALU.add)\
                        .then_inc(ty.sem("conv_done"), 1)
                    dve.wait_ge(ty.sem("conv_squared"), n + 1)
                    step(dve.tensor_scalar(inner, work, GELU_B, 1.0, ALU.mult, ALU.add), 3)
                    dve.tensor_tensor(inner, inner, conv, ALU.mult).then_inc(ty.sem("act_in"), 1)
                    dve.wait_ge(ty.sem("act_tanh"), n + 1)
                    step(dve.scalar_tensor_tensor(out=inner, in0=work, scalar=1.0, in1=conv,
                                                  op0=ALU.add, op1=ALU.mult), 4)
                    dve.scalar_tensor_tensor(out=full_, in0=inner, scalar=0.5, in1=ps[:, 1, :],
                                             op0=ALU.mult, op1=ALU.mult).then_inc(ty.sem("act_full"), 1)
                    dve.wait_ge(ty.sem("act_high"), n + 1)
                    dve.tensor_tensor(actl[:, n, :], full_, acth[:, n, :].bitcast(F32), ALU.subtract)\
                        .then_inc(ty.sem("act_low"), 1)

            with dve.Fori(0, FC // 2) as i:
                gate_up(i)

            norm("mpost", y, lambda k: tmp[:, 2 + k % 2, 0:S], seq, vcol(V_MPOST), rstd[:, 0:S])
            dve.wait_ge(*at("p_high", 0))
            dve.tensor_tensor(pl[:], pT[:], ph[:].bitcast(F32), ALU.subtract).then_inc(*tick("p_low", 0))
            for k in range(DC):
                dve.wait_ge(*at("x_high", k))
                dve.tensor_tensor(hl[:, k, 0:S], x[:, k, seq], hh[:, k, 0:S].bitcast(F32), ALU.subtract)\
                    .then_inc(*tick("x_low", k))
            for m in range(DC):
                dve.wait_ge(*at("ple_tanh", m))
                if m >= 2:
                    dve.wait_ge(*at("x_new", ("ple", m - 2)))
                dve.scalar_tensor_tensor(out=tmp[:, 2 + m % 2, 0:S], in0=tmp[:, m % 2, 0:S], scalar=1.0,
                                         in1=(G, S0)[m % 2][:, 1, :], op0=ALU.add, op1=ALU.mult)\
                    .then_inc(*tick("ple_step", m))
                dve.wait_ge(*at("ple_step", m))
                dve.scalar_tensor_tensor(out=x[:, m, seq], in0=tmp[:, 2 + m % 2, 0:S], scalar=0.5,
                                         in1=x[:, m, seq], op0=ALU.mult, op1=ALU.add)\
                    .then_inc(*tick("x_new", ("ple", m)))

            with dve.Fori(0, LAYERS) as l:
                ty.enter("layer", l, LAYERS)
                steps = [0]

                def chain(ins, alone=False):
                    steps[0] += 1
                    ins.then_inc(*tick("dve_step", steps[0]))
                    dve.wait_ge(*at("dve_step", steps[0]))
                    if alone:
                        hold(dve)

                cos, sin = const[:, C_COS:C_COS + T], const[:, C_SIN:C_SIN + T]
                dve.wait_ge(*at("lvec_in", 0))
                norm("layer", lambda k: x[:, k, :], lambda k: probs2[:, 2 + k % 2, :], slice(0, T),
                     lambda k: lvec[:, W_NORM + k:W_NORM + k + 1], score[:, 0, :],
                     (lambda k: hh[:, k, :], lambda k: hl[:, k, :]))

                chain(dve.memset(pool3[:, :, 0:META], 0.0))
                dve.wait_ge(*at("k_rms", 0))
                dve.reciprocal(score[:, 1, :], score[:, 0, :])
                dve.tensor_tensor(probs2[:, 2, :], probs2[:, 1, :], cos, ALU.mult)
                dve.wait_ge(*at("k_turned", 0))
                chain(dve.tensor_tensor(halves(probs2[:, 3, :]), full(S0), halves(sin), ALU.mult))
                dve.tensor_tensor(probs2[:, 2, :], probs2[:, 2, :], probs2[:, 3, :], ALU.add)\
                    .then_inc(*tick("k_ready", 0))
                dve.wait_ge(*at("k_ready", 0))
                for half in range(2):
                    dve.tensor_tensor(kT2[half * HD:(half + 1) * HD, :], probs2[0:HD, 2, :], score[0:HD, 1, :],
                                      ALU.mult)
                    ins = dve.tensor_copy(kiT2[half * HD:(half + 1) * HD, :], probs2[HD:P, 2, :])
                ins.then_inc(*tick("k_ready", 1))
                for c in range(8):
                    buf = (qi2, q2)[c >= 4][:, c % 4, :]
                    dve.wait_ge(*at("q_raw", c))
                    dve.wait_ge(*(at("q_ready", c - 1) if c else at("k_ready", 1)))
                    dve.tensor_tensor(probs2[:, 2, :], buf, cos, ALU.mult)
                    dve.wait_ge(*at("q_turned", c))
                    chain(dve.tensor_tensor(halves(probs2[:, 3, :]), full((S0, S1)[c % 2]), halves(sin), ALU.mult))
                    dve.tensor_tensor(buf, probs2[:, 2, :], probs2[:, 3, :], ALU.add)\
                        .then_inc(*tick("q_ready", c))
                dve.wait_ge(*at("rq_rms", 0))
                dve.reciprocal(rq[0:META, 1, 0, :], rq[0:META, 0, 0, :])
                chain(dve.reciprocal(rq[:, 1, 1:, :], rq[:, 0, 1:, :]))
                dve.tensor_scalar(rq[0:META, 2, 0, :], rq[0:META, 1, 0, :], SCALE, None, ALU.mult)
                dve.tensor_scalar(rq[:, 2, 1:, :], rq[:, 1, 1:, :], SCALE, None, ALU.mult)\
                    .then_inc(*tick("rq", 0))
                chain(dve.memset(keep[0:META, 0:META], 0.0))
                dve.wait_ge(*at("rq", 0))

                def fill(kind, c):
                    if kind == "gb":
                        dve.wait_ge(*at("gateb_tanh", c))
                        dve.scalar_tensor_tensor(out=halves(gateb), in0=halves(gateb), scalar=1.0, in1=full(G),
                                                 op0=ALU.add, op1=ALU.mult).then_inc(*tick("g_read_d", (kind, c)))
                    elif kind == "ga":
                        dve.wait_ge(*at("gatea_tanh", c))
                        dve.scalar_tensor_tensor(out=halves(sila[:, c, :]), in0=halves(sila[:, c, :]), scalar=1.0,
                                                 in1=full(G), op0=ALU.add, op1=ALU.mult)\
                            .then_inc(*tick("g_read_d", (kind, c)))
                    elif kind == "ub":
                        dve.wait_ge(*at("g_read_a", (kind, c)))
                        src = 0
                        for e in range(c + 1):
                            dst = 1 + e % 2
                            w = 2 ** e
                            chain(dve.tensor_tensor(pool3[:, dst, META:META + T], pool3[:, src, META:META + T],
                                                    pool3[:, src, META - w:META + T - w], ALU.add))
                            src = dst
                        w = 2 ** (c + 1)
                        assert src != 2 - c % 2
                        out = pooled(c)
                        a, u = pool3[:, src, META:META + T], pool3[:, 0, META:META + T]
                        dve.scalar_tensor_tensor(out=out[:, META:T], in0=a[:, META:T], scalar=1.0 / w,
                                                 in1=u[:, META:T], op0=ALU.mult, op1=ALU.subtract)
                        cnt = const[:, C_CNT + c * META:C_CNT + (c + 1) * META]
                        chain(dve.tensor_tensor(out[:, 0:META], a[:, 0:META], cnt, ALU.mult))
                        dve.tensor_tensor(out[:, 0:META], out[:, 0:META], u[:, 0:META], ALU.subtract)\
                            .then_inc(*tick("pooled", c))
                        dve.wait_ge(*at("pool_mixed", c))
                        dve.tensor_scalar(halves(u), full(G), lvec[:, W_PB + c:W_PB + c + 1],
                                          lvec[:, W_PS + c:W_PS + c + 1], ALU.add, ALU.mult)\
                            .then_inc(*tick("g_read_d", ("pm", c)))
                        dve.wait_ge(*at("g_read_d", ("pm", c)))
                        b = pool3[:, 1, META:META + T]
                        dve.scalar_tensor_tensor(out=b, in0=u, scalar=0.5, in1=gateb, op0=ALU.mult, op1=ALU.mult)\
                            .then_inc(*tick("branch_b", c))
                        dve.wait_ge(*at("b_high", c))
                        dve.tensor_tensor(bl[:, c, :], b, bh[:, c, :].bitcast(F32), ALU.subtract)\
                            .then_inc(*tick("b_low", c))

                for j in range(QT + 1):
                    t0, m = rows2(j)
                    n = seen2(j)
                    if j:
                        sc = score[0:m, 0, 0:n]
                        for h in range(HEADS):
                            dve.wait_ge(*at("relued", (j, h)))
                            wh = v2[0:m, j, HD + h:HD + h + 1]
                            rl = relu[0:m, h % 2, 0:n]
                            if h == 0:
                                ins = dve.tensor_scalar(sc, rl, wh, None, ALU.mult)
                            else:
                                ins = dve.scalar_tensor_tensor(out=sc, in0=rl, scalar=wh, in1=sc, op0=ALU.mult,
                                                               op1=ALU.add)
                            ins.then_inc(*tick("indexed", (j, h)))
                            dve.wait_ge(*at("indexed", (j, h)))
                        vis = const[:, C_VIS:C_VIS + HD]
                        chain(dve.tensor_tensor(sc[:, n - HD:n], sc[:, n - HD:n], vis, ALU.add), alone=True)
                        fills = filler[j]
                        done = 0
                        for rnd in range(TOPK // 8):
                            chain(dve.max(top8[:], sc), alone=True)
                            chain(dve.match_replace(out=sc, in_to_replace=top8[:], in_values=sc, imm_value=-3e38),
                                  alone=True)
                            while done < len(fills) and done * (TOPK // 8) < (rnd + 1) * len(fills):
                                fill(*fills[done])
                                done += 1
                        chain(dve.tensor_scalar(keep[:, 0:n], sc, -2e38, -BIG, ALU.is_gt, ALU.mult))
                        chain(dve.tensor_tensor(keep[:, n - HD:n], keep[:, n - HD:n], vis, ALU.add))
                    else:
                        for f in filler[j]:
                            fill(*f)
                    for half in range(2):
                        st = small[0:m, :, :]
                        for r in range(REP):
                            if r == 0 and (j or half):
                                dve.wait_ge(*at("weighed2", turns2[j, half]))
                            dve.wait_ge(*at("scored2", (j, half, r)))
                            hold(dve)
                            ps = (S0, S1)[bank_of[("masked", (j, half, r))]]
                            dve.tensor_tensor_reduce(wide(probs2[0:m, r, 0:n], n), scores2(ps, m, n),
                                                     wide(keep[0:m, 0:n], n), 1.0, -3e38, ALU.add, ALU.max,
                                                     st[:, 0, r:r + 1]).then_inc(*tick("masked", (j, half, r)))
                        dve.wait_ge(*at("masked", (j, half, REP - 1)))
                        dve.scalar_tensor_tensor(out=st[:, 1, 0:REP], in0=st[:, 0, 0:REP], scalar=-1.0,
                                                 in1=rq[0:m, 2, j, half * REP:(half + 1) * REP], op0=ALU.mult,
                                                 op1=ALU.mult).then_inc(*tick("neg_max2", (j, half)))
                        dve.wait_ge(*at("exped2", (j, half, REP - 1)))
                        chain(dve.reciprocal(st[:, 3, 0:REP], st[:, 2, 0:REP]))
                        for r in range(REP):
                            pr = probs2[0:m, r, 0:n]
                            dve.tensor_scalar(pr, pr, st[:, 3, r:r + 1], None, ALU.mult)\
                                .then_inc(*tick("weighted2", (j, half, r)))
                        dve.wait_ge(*at("weighed2", turns2[(j, 1) if half == 0 else (j + 1, 0)]))
                        if j or half:
                            dve.wait_ge(*at("a_low", (j, 0) if half else (j - 1, 1)))
                        if (j, half) == (0, 0):
                            dve.wait_ge(*at("g_read_d", ("ga", 3)))
                        dve.scalar_tensor_tensor(out=relu[:, 0:2, 0:m],
                                                 in0=X[:, 1, 0:2 * m].rearrange("p (c q) -> p c q", c=2), scalar=0.5,
                                                 in1=sila[:, 2 * half:2 * half + 2, t0:t0 + m], op0=ALU.mult,
                                                 op1=ALU.mult).then_inc(*tick("gated_a", (j, half)))
                        dve.wait_ge(*at("a_high", (j, half)))
                        sel = (slice(None), slice(2 * half, 2 * half + 2), slice(t0, t0 + m))
                        dve.tensor_tensor(al[sel], relu[:, 0:2, 0:m], ah[sel].bitcast(F32), ALU.subtract)\
                            .then_inc(*tick("a_low", (j, half)))

                for k in range(DC):
                    pair = (G, S0) if k % 2 == 0 else (S1, X)
                    dve.wait_ge(ty.sem("unit_used"), l * L_UNITS + (U_LAYER + L_WAB + k + 1))
                    a, b = merge[:, k, :], merge[:, DC + k, :]
                    dve.scalar_tensor_tensor(out=halves(a), in0=halves(a), scalar=1.0, in1=full(pair[0]),
                                             op0=ALU.add, op1=ALU.mult)
                    chain(dve.scalar_tensor_tensor(out=halves(b), in0=halves(b), scalar=1.0, in1=full(pair[1]),
                                                   op0=ALU.add, op1=ALU.mult))
                    dve.tensor_tensor(a, a, b, ALU.add).then_inc(*tick("merged", k))
                    dve.wait_ge(*at("z_high", k))
                    dve.scalar_tensor_tensor(out=hl[:, k, :], in0=a, scalar=0.5, in1=hh[:, k, :].bitcast(F32),
                                             op0=ALU.mult, op1=ALU.subtract).then_inc(*tick("z_low", k))
                for k in range(DC):
                    dve.wait_ge(ty.sem("unit_used"), l * L_UNITS + (U_LAYER + L_OUT + k + 1))
                    dve.tensor_tensor(halves(x[:, k, :]), halves(x[:, k, :]), full((G, S0)[k % 2]), ALU.add)\
                        .then_inc(*tick("x_new", ("layer", k)))
                ty.leave()
    return ty


def constants():
    c = np.zeros((P, NC_CONST), np.float32)
    p = np.arange(P)[:, None]
    c[:, C_ID:C_ID + P] = np.eye(P)
    c[:, C_ONES:C_ONES + P] = 1
    c[:, C_BONES:C_BONES + P] = p // HD == np.arange(P)[None] // HD
    for i in range(P):
        if i % HD < HD // 2:
            c[i + HD // 2, C_ROT + i] = -1
        else:
            c[i - HD // 2, C_ROT + i] = 1
    inv = np.float32(1) / (np.float32(10000) ** (np.arange(0, HD, 2, dtype=np.float32) / np.float32(HD)))
    ang = np.arange(T, dtype=np.float32)[:, None] * inv[None, :]
    ang = np.concatenate([ang] * 4, axis=1).T
    c[:, C_COS:C_COS + T] = np.cos(ang)
    c[:, C_SIN:C_SIN + T] = np.sin(ang)
    dist = p + 384 - np.arange(S)[None]
    c[:, C_DIST:C_DIST + S] = np.where(dist >= 0, dist, BIG)
    dist = P + p - np.arange(2 * P)[None]
    c[:, C_SDIST:C_SDIST + 2 * P] = np.where((dist >= 0) & (dist < P), dist, BIG)
    for t in range(QT):
        dist = t * P + p - (np.arange(NCMP)[None] * CMP_STRIDE + 31)
        c[:, C_CDIST + 32 * t:C_CDIST + 32 * t + NCMP] = np.where(dist >= 0, dist, BIG)
        c[:, C_SOME + t] = (t * P + p[:, 0]) >= 31
    for g in range(POOL_C):
        c[:, C_CNT + g * META:C_CNT + (g + 1) * META] = 1 / np.minimum(np.arange(1, META + 1), 2 ** (g + 1))
    c[0:HD, C_VIS:C_VIS + HD] = -BIG
    c[:, C_EPS] = EPS
    return c


def tiles(w):
    k, m = w.shape
    return w.reshape(k // P, P, m // P, P).transpose(2, 1, 0, 3)


def packed(w):
    t = tiles(w).transpose(0, 2, 1, 3).reshape(-1, 8, P, P)
    return t.transpose(0, 2, 1, 3)


def columns(v):
    return v.reshape(-1, P).T


def layout(a):
    w = a["w_in"][0]
    q_s = 1304
    cols = [slice(512, 640), slice(640, 768), slice(768, 896), slice(1024, 1152), slice(1816, 1944),
            slice(896, 1024), slice(1152, 1280), slice(1944, 2072)]
    units = [tiles(w[:, c]) for c in cols] + [tiles(w[:, 0:512]), tiles(w[:, q_s:q_s + 512])]
    units.append(tiles(a["w_o"][0]))
    gu = tiles(a["w_gate_up"][0]).reshape(2, FC, P, 8, P).transpose(1, 0, 2, 3, 4).reshape(2 * FC, P, 8, P)
    units.append(gu)
    units.append(packed(a["w_down"][0]))
    units.append(packed(np.concatenate([a["w_ple_gate"][0], a["w_ple"][0]], axis=0)))
    for l in range(LAYERS):
        w = a["w_in_2"][l]
        pad = np.zeros((D, P - 72), w.dtype)
        units.append(tiles(np.concatenate([w[:, 512:576], w[:, 2688:2752]], axis=1)))
        units.append(tiles(np.concatenate([w[:, 576:640], w[:, 2752:2760], pad], axis=1)))
        units += [tiles(w[:, 2176:2688]), tiles(w[:, 0:512]), tiles(w[:, 640:1152])]
        gb, ub = tiles(w[:, 1664:2176]), tiles(w[:, 1152:1664])
        units.append(np.stack([gb, ub], axis=1).reshape(8, P, 8, P))
        units.append(tiles(w[:, 2760:4808]))
        units.append(tiles(np.concatenate([a["w_branch_a_2"][l], a["w_branch_b_2"][l]], axis=0)))
        units.append(tiles(a["w_out_2"][l]))
    stream = np.concatenate(units, axis=0)
    assert stream.shape == (UNITS, P, DC, P)

    vec = np.concatenate([
        columns(a["attn_pre_g"][0]), columns(a["attn_post_g"][0]), columns(a["mlp_pre_g"][0]),
        columns(a["mlp_post_g"][0]), columns(a["conv_w"][0]), columns(a["conv_b"][0]),
        columns(a["cmp_pe_k"][0]), columns(a["cmp_pe_v"][0]), np.broadcast_to(a["sinks"][0][None], (P, HEADS)),
    ], axis=1)
    lvec = np.stack([np.concatenate([
        columns(a["norm_gain_2"][l]), np.tile(a["q_norm_gain_2"][l], 2)[:, None],
        np.concatenate([a["k_norm_gain_2"][l], np.ones(HD, np.float32)])[:, None],
        columns(a["pool_b_2"][l]), columns(a["pool_scale_2"][l]),
    ], axis=1) for l in range(LAYERS)])

    def chunked(rows):
        return rows.reshape(rows.shape[0], -1, P).transpose(2, 1, 0)

    out = {
        "x": chunked(a["x"][0]), "meta": chunked(a["meta_tokens_2"]), "p": chunked(a["p"][0, 0]),
        "w": stream, "const": constants(), "vec": vec, "lvec": lvec,
        "poolw": a["pool_w_2"].transpose(0, 2, 1, 3),
        "wg": a["w_in"][0][:, 1280:1304].reshape(DC, P, 24).transpose(1, 0, 2),
    }
    for n in "kv":
        out["cw1" + n] = a["cmp_w1_" + n][0].reshape(16, P, P).transpose(1, 0, 2)
        out["cw2" + n] = np.concatenate([a["cmp_w2_" + n][0]] * 2, axis=1)
    return {n: np.ascontiguousarray(v) for n, v in out.items()}


def kernel(**inputs):
    from concourse.bacc import Bacc
    from concourse.bass_utils import run_bass_kernel_spmd

    arrays = layout({n: np.asarray(v) for n, v in inputs.items()})

    def program(known):
        nc = Bacc("TRN2", target_bir_lowering=False, num_devices=1)
        io = {n: nc.dram_tensor("in_" + n, v.shape, mybir.dt.from_np(v.dtype), kind="ExternalInput").ap()
              for n, v in arrays.items()}
        io["out"] = nc.dram_tensor("out_0", (P, DC, S), F32, kind="ExternalOutput").ap()
        return nc, build(nc, io, known)

    _, counted = program(None)
    nc, _ = program(counted)
    r = run_bass_kernel_spmd(nc, [{"in_" + n: v for n, v in arrays.items()}], core_ids=[0])
    out = r.results[0]["out_0"]
    return np.ascontiguousarray(out.transpose(2, 1, 0).reshape(1, S, D))
```
